# Optimizing a Trainium2 kernel written in Bass

```python
import math
import jax
import jax.numpy as jnp
from jax import lax
import numpy as np

D_MODEL = 2048
BATCH = 1
SEQ = 256
DEPTH = 2
DEC_BATCH = 8
DEC_SEQ = 1
PAST_LEN = 2048
PAGE_SIZE = 128

MIX_WIDTH = D_MODEL
RET_WIDTH = 3 * D_MODEL // 8
MLSTM_WIDTH = 3 * D_MODEL // 8
POOL_WIDTH = MIX_WIDTH - RET_WIDTH - MLSTM_WIDTH
RET_HEADS = 6
RET_HEAD_DIM = RET_WIDTH // RET_HEADS
MLSTM_HEADS = 4
MLSTM_V_DIM = MLSTM_WIDTH // MLSTM_HEADS
MLSTM_QK_DIM = MLSTM_V_DIM // 2
POOL_WINDOWS = (2, 4, 8, 16)
POOL_GROUPS = len(POOL_WINDOWS)
POOL_GROUP_WIDTH = POOL_WIDTH // POOL_GROUPS
POOL_BUF = max(POOL_WINDOWS) - 1
D_FF = ((8 * D_MODEL + 3 * 256 - 1) // (3 * 256)) * 256
CHUNK = 128
ROPE_THETA = 10000.0
EPS = 1e-6
IN_SPLITS = (RET_WIDTH, RET_WIDTH, RET_WIDTH, RET_WIDTH,
             MLSTM_HEADS * MLSTM_QK_DIM, MLSTM_HEADS * MLSTM_QK_DIM,
             MLSTM_WIDTH, MLSTM_WIDTH, MLSTM_HEADS, MLSTM_HEADS, POOL_WIDTH)
IN_WIDTH = sum(IN_SPLITS)

kernel_name = 'hybrid_retention_mlstm_pool_step'

def _rms_norm(x, g):
    xf = x.astype(jnp.float32)
    y = xf * lax.rsqrt(jnp.mean(xf * xf, axis=-1, keepdims=True) + EPS)
    return (y * g.astype(jnp.float32)).astype(x.dtype)

def _head_rms_norm(x, g):
    b, l, h, d = x.shape
    y = x * lax.rsqrt(jnp.mean(x * x, axis=-1, keepdims=True) + EPS)
    return y.reshape(b, l, h * d) * g.astype(jnp.float32)

def _rotary(x, pos):
    half = x.shape[-1] // 2
    inv_freq = ROPE_THETA ** (-jnp.arange(half, dtype=jnp.float32) / half)
    ang = pos[:, None] * inv_freq[None, :]
    cos = jnp.cos(ang)[None, :, None, :]
    sin = jnp.sin(ang)[None, :, None, :]
    x1, x2 = x[..., :half], x[..., half:]
    return jnp.concatenate([x1 * cos - x2 * sin, x1 * sin + x2 * cos], axis=-1)

def _chunk_len(length):
    return length if length <= CHUNK else math.gcd(length, CHUNK)

def _to_chunks(t, c):
    b, l = t.shape[:2]
    t = t.reshape((b, l // c, c) + t.shape[2:])
    return jnp.swapaxes(jnp.moveaxis(t, 1, 0), 2, 3)

def _from_chunks(t):
    n, b, h, c, d = t.shape
    return jnp.moveaxis(jnp.swapaxes(t, 2, 3), 0, 1).reshape(b, n * c, h, d)

def _retention(q, k, v, s0, log_gamma):
    c = _chunk_len(q.shape[1])
    qc, kc, vc = (_to_chunks(t, c) for t in (q, k, v))
    idx = jnp.arange(c, dtype=jnp.float32)
    diff = idx[:, None] - idx[None, :]
    causal = diff >= 0
    lg = log_gamma[:, None, None]
    decay_intra = jnp.where(causal, jnp.exp(lg * jnp.where(causal, diff, 0.0)), 0.0)
    decay_q = jnp.exp(log_gamma[:, None] * (idx + 1.0))[None, :, :, None]
    decay_k = jnp.exp(log_gamma[:, None] * (c - 1.0 - idx))[None, :, :, None]
    decay_chunk = jnp.exp(log_gamma * c)[None, :, None, None]

    def step(s, inp):
        qi, ki, vi = inp
        scores = jnp.einsum('bhid,bhjd->bhij', qi, ki) * decay_intra
        o = (jnp.einsum('bhij,bhjv->bhiv', scores, vi)
             + jnp.einsum('bhid,bhdv->bhiv', qi, s) * decay_q)
        s_new = s * decay_chunk + jnp.einsum('bhjd,bhjv->bhdv', ki * decay_k, vi)
        return s_new, o

    s_fin, o = lax.scan(step, s0.astype(jnp.float32), (qc, kc, vc))
    return _from_chunks(o), s_fin

def _mlstm(q, k, v, i_pre, logf, c0, n0, m0):
    c = _chunk_len(q.shape[1])
    qc, kc, vc, ic, fc = (_to_chunks(t, c) for t in (q, k, v, i_pre, logf))
    causal = jnp.tril(jnp.ones((c, c), dtype=bool))

    def step(carry, inp):
        cm, nv, m = carry
        qi, ki, vi, ii, lf = inp
        b = jnp.cumsum(lf, axis=-1)
        logw = jnp.where(causal, b[..., :, None] - b[..., None, :] + ii[..., None, :], -jnp.inf)
        inter = b + m[..., None]
        m_t = jnp.maximum(inter, jnp.max(logw, axis=-1))
        w = jnp.exp(logw - m_t[..., None])
        a = jnp.exp(inter - m_t)
        s = jnp.einsum('bhtd,bhjd->bhtj', qi, ki) * w
        num = (jnp.einsum('bhtj,bhjv->bhtv', s, vi)
               + a[..., None] * jnp.einsum('bhtd,bhdv->bhtv', qi, cm))
        den = jnp.sum(s, axis=-1) + a * jnp.einsum('bhtd,bhd->bht', qi, nv)
        h = num / jnp.maximum(jnp.abs(den), jnp.exp(-m_t))[..., None]
        m_new = m_t[..., -1]
        wk = jnp.exp(b[..., -1:] - b + ii - m_new[..., None])[..., None] * ki
        a_end = jnp.exp(b[..., -1] + m - m_new)
        cm_new = a_end[..., None, None] * cm + jnp.einsum('bhjd,bhjv->bhdv', wk, vi)
        nv_new = a_end[..., None] * nv + jnp.sum(wk, axis=2)
        return (cm_new, nv_new, m_new), h

    f32 = jnp.float32
    (cf, nf, mf), h = lax.scan(step, (c0.astype(f32), n0.astype(f32), m0.astype(f32)),
                               (qc, kc, vc, ic, fc))
    return _from_chunks(h), cf, nf, mf

def _pool_mixer(u, buf, pos, w_pool, pool_scale):
    b, l, p = u.shape
    f32 = jnp.float32
    full = jnp.concatenate([buf.astype(f32), u], axis=1)
    cs = jnp.concatenate([jnp.zeros((b, 1, p), f32), jnp.cumsum(full, axis=1)], axis=1)
    upper = cs[:, POOL_BUF + 1:, :]
    z = []
    for g, win in enumerate(POOL_WINDOWS):
        sl = slice(g * POOL_GROUP_WIDTH, (g + 1) * POOL_GROUP_WIDTH)
        lower = cs[:, POOL_BUF + 1 - win:POOL_BUF + 1 - win + l, sl]
        count = jnp.minimum(pos + 1.0, float(win))[None, :, None]
        z.append((upper[..., sl] - lower) / count - u[..., sl])
    z = jnp.stack(z, axis=2)
    y = jnp.einsum('blgc,gce->blge', z, w_pool.astype(f32)).reshape(b, l, p)
    return y * pool_scale.astype(f32), full[:, -POOL_BUF:, :]

def _layer(x, pos, s_ret, s_c, s_n, s_m, s_pool,
           w_in, w_out, g_ret_norm, g_mlstm_norm, b_mlstm_i, b_mlstm_f, w_pool, pool_scale,
           g_pre_mix, g_post_mix, g_pre_ffn, g_post_ffn, w_ffn_gate, w_ffn_up, w_ffn_down):
    b, l, _ = x.shape
    f32 = jnp.float32
    xn = _rms_norm(x, g_pre_mix)
    proj = xn @ w_in
    parts = []
    start = 0
    for width in IN_SPLITS:
        parts.append(proj[..., start:start + width].astype(f32))
        start += width
    rq, rk, rv, rg, mq, mk, mv, mo, mi, mf, pu = parts

    rq = _rotary(rq.reshape(b, l, RET_HEADS, RET_HEAD_DIM), pos)
    rk = _rotary(rk.reshape(b, l, RET_HEADS, RET_HEAD_DIM), pos) * RET_HEAD_DIM ** -0.5
    rv = rv.reshape(b, l, RET_HEADS, RET_HEAD_DIM)
    log_gamma = jnp.log1p(-jnp.exp2(-5.0 - jnp.arange(RET_HEADS, dtype=f32)))
    ro, s_ret_new = _retention(rq, rk, rv, s_ret, log_gamma)
    ret_out = _head_rms_norm(ro, g_ret_norm) * jax.nn.silu(rg)

    mq = mq.reshape(b, l, MLSTM_HEADS, MLSTM_QK_DIM)
    mk = mk.reshape(b, l, MLSTM_HEADS, MLSTM_QK_DIM) * MLSTM_QK_DIM ** -0.5
    mv = mv.reshape(b, l, MLSTM_HEADS, MLSTM_V_DIM)
    i_pre = mi + b_mlstm_i.astype(f32)
    logf = jax.nn.log_sigmoid(mf + b_mlstm_f.astype(f32))
    mh, c_new, n_new, m_new = _mlstm(mq, mk, mv, i_pre, logf, s_c, s_n, s_m)
    mlstm_out = _head_rms_norm(mh, g_mlstm_norm) * jax.nn.sigmoid(mo)

    pool_out, pool_new = _pool_mixer(pu, s_pool, pos, w_pool, pool_scale)

    mixed = jnp.concatenate([ret_out, mlstm_out, pool_out], axis=-1).astype(x.dtype) @ w_out
    x = x + _rms_norm(mixed, g_post_mix)
    hn = _rms_norm(x, g_pre_ffn)
    ff = (jax.nn.silu(hn @ w_ffn_gate) * (hn @ w_ffn_up)) @ w_ffn_down
    x = x + _rms_norm(ff, g_post_ffn)
    return x, (s_ret_new, c_new, n_new, m_new, pool_new)

def setup_inputs(seed: int = 0) -> dict:
    key = jax.random.key(seed)
    ks = jax.random.split(key, 24)
    f32 = jnp.float32

    def nrm(k, shape, scale):
        return scale * jax.random.normal(k, shape, f32)

    def gain(k, shape):
        return 1.0 + 0.1 * jax.random.normal(k, shape, f32)

    return {
        'x_prompt': nrm(ks[0], (BATCH, SEQ, D_MODEL), 1.0),
        'x_sample': nrm(ks[1], (DEC_BATCH, DEC_SEQ, D_MODEL), 1.0),
        'state_ret': nrm(ks[2], (DEPTH, DEC_BATCH, RET_HEADS, RET_HEAD_DIM, RET_HEAD_DIM), RET_HEAD_DIM ** -0.5),
        'state_mlstm_c': nrm(ks[3], (DEPTH, DEC_BATCH, MLSTM_HEADS, MLSTM_QK_DIM, MLSTM_V_DIM), 0.5),
        'state_mlstm_n': nrm(ks[4], (DEPTH, DEC_BATCH, MLSTM_HEADS, MLSTM_QK_DIM), 0.5),
        'state_mlstm_m': nrm(ks[5], (DEPTH, DEC_BATCH, MLSTM_HEADS), 1.0),
        'state_pool': nrm(ks[6], (DEPTH, DEC_BATCH, POOL_BUF, POOL_WIDTH), 1.0),
        'w_in': nrm(ks[7], (DEPTH, D_MODEL, IN_WIDTH), D_MODEL ** -0.5),
        'w_out': nrm(ks[8], (DEPTH, MIX_WIDTH, D_MODEL), MIX_WIDTH ** -0.5),
        'g_ret_norm': gain(ks[9], (DEPTH, RET_WIDTH)),
        'g_mlstm_norm': gain(ks[10], (DEPTH, MLSTM_WIDTH)),
        'b_mlstm_i': nrm(ks[11], (DEPTH, MLSTM_HEADS), 0.1),
        'b_mlstm_f': jnp.linspace(3.0, 6.0, MLSTM_HEADS, dtype=f32)[None, :] + nrm(ks[12], (DEPTH, MLSTM_HEADS), 0.1),
        'w_pool': nrm(ks[13], (DEPTH, POOL_GROUPS, POOL_GROUP_WIDTH, POOL_GROUP_WIDTH), POOL_GROUP_WIDTH ** -0.5),
        'pool_scale': gain(ks[14], (DEPTH, POOL_WIDTH)),
        'g_pre_mix': gain(ks[15], (DEPTH, D_MODEL)),
        'g_post_mix': gain(ks[16], (DEPTH, D_MODEL)),
        'g_pre_ffn': gain(ks[17], (DEPTH, D_MODEL)),
        'g_post_ffn': gain(ks[18], (DEPTH, D_MODEL)),
        'w_ffn_gate': nrm(ks[19], (DEPTH, D_MODEL, D_FF), D_MODEL ** -0.5),
        'w_ffn_up': nrm(ks[20], (DEPTH, D_MODEL, D_FF), D_MODEL ** -0.5),
        'w_ffn_down': nrm(ks[21], (DEPTH, D_FF, D_MODEL), D_FF ** -0.5),
    }

def reference(x_prompt, x_sample, state_ret, state_mlstm_c, state_mlstm_n, state_mlstm_m, state_pool,
              w_in, w_out, g_ret_norm, g_mlstm_norm, b_mlstm_i, b_mlstm_f, w_pool, pool_scale,
              g_pre_mix, g_post_mix, g_pre_ffn, g_post_ffn, w_ffn_gate, w_ffn_up, w_ffn_down):
    f32 = jnp.float32
    bp, lp, _ = x_prompt.shape
    pos_prompt = jnp.arange(lp, dtype=f32)
    pos_sample = (PAST_LEN + jnp.arange(x_sample.shape[1])).astype(f32)
    zero_ret = jnp.zeros((bp, RET_HEADS, RET_HEAD_DIM, RET_HEAD_DIM), f32)
    zero_c = jnp.zeros((bp, MLSTM_HEADS, MLSTM_QK_DIM, MLSTM_V_DIM), f32)
    zero_n = jnp.zeros((bp, MLSTM_HEADS, MLSTM_QK_DIM), f32)
    zero_m = jnp.zeros((bp, MLSTM_HEADS), f32)
    zero_pool = jnp.zeros((bp, POOL_BUF, POOL_WIDTH), f32)

    y_prompt, y_sample = x_prompt, x_sample
    new_p, new_s = [], []
    for layer in range(DEPTH):
        params = (w_in[layer], w_out[layer], g_ret_norm[layer], g_mlstm_norm[layer],
                  b_mlstm_i[layer], b_mlstm_f[layer], w_pool[layer], pool_scale[layer],
                  g_pre_mix[layer], g_post_mix[layer], g_pre_ffn[layer], g_post_ffn[layer],
                  w_ffn_gate[layer], w_ffn_up[layer], w_ffn_down[layer])
        y_prompt, st_p = _layer(y_prompt, pos_prompt, zero_ret, zero_c, zero_n, zero_m, zero_pool, *params)
        y_sample, st_s = _layer(y_sample, pos_sample, state_ret[layer], state_mlstm_c[layer],
                                state_mlstm_n[layer], state_mlstm_m[layer], state_pool[layer], *params)
        new_p.append(st_p)
        new_s.append(st_s)

    def stack(states, i, dtype):
        return jnp.stack([s[i] for s in states], axis=0).astype(dtype)

    ret_p = stack(new_p, 0, state_ret.dtype)
    c_p = stack(new_p, 1, state_mlstm_c.dtype)
    n_p = stack(new_p, 2, state_mlstm_n.dtype)
    m_p = stack(new_p, 3, state_mlstm_m.dtype)
    pool_p = stack(new_p, 4, state_pool.dtype)
    ret_s = stack(new_s, 0, state_ret.dtype)
    c_s = stack(new_s, 1, state_mlstm_c.dtype)
    n_s = stack(new_s, 2, state_mlstm_n.dtype)
    m_s = stack(new_s, 3, state_mlstm_m.dtype)
    pool_s = stack(new_s, 4, state_pool.dtype)
    return (y_prompt, y_sample, ret_p, c_p, n_p, m_p, pool_p, ret_s, c_s, n_s, m_s, pool_s)


_drawn_inputs = setup_inputs


def setup_inputs(seed=0):
    import zlib

    import numpy as np

    out = dict(_drawn_inputs(seed))
    spreads = {}
    factors = {}
    for name, (base, spread) in spreads.items():
        noise = np.random.default_rng([zlib.crc32(name.encode()), seed]).standard_normal(out[name].shape)
        drawn = base * np.exp(spread * noise) if base else spread * noise
        out[name] = jnp.asarray(drawn.astype(out[name].dtype))
    for name, factor in factors.items():
        out[name] = (out[name] * factor).astype(out[name].dtype)
    return out
```

```python
from contextlib import ExitStack

import numpy as np
import concourse.bass as bass
from concourse import mybir

F32 = mybir.dt.float32
F32R = mybir.dt.float32r
ALU = mybir.AluOpType
ACT = mybir.ActivationFunctionType
AX = mybir.AxisListType

P = 128
D_MODEL, BATCH_S, SEQ, DEPTH, PAST = 2048, 8, 256, 2, 2048
TOK = SEQ + BATCH_S
CH = 128
KT = D_MODEL // P
RH, RD = 6, 128
MH, MQK, MV = 4, 96, 192
PG, PBUF = 4, 15
D_FF = ((8 * D_MODEL + 3 * 256 - 1) // (3 * 256)) * 256
FT = D_FF // P
NBLK = 2
BT = FT // NBLK
HT = BT // 2
EPS = 1e-6

T_RQ, T_RK, T_RV, T_RG, T_MQ, T_MK, T_MV, T_MO, T_PU = 0, 6, 12, 18, 24, 28, 32, 38, 44
NPROJ = 48
X_RET, X_ML, X_POOL = 0, 6, 12

CHUNK = KT * P
HALF = HT * P
C_IN, C_OUT = 0, NPROJ
C_GU = [64, 140]
C_DN = [108, 184]
N_CHUNKS = 216
O_IN, O_OUT = 0, 48
O_GU = [64, 124]
O_DN = [108, 168]
N_TILES = 184
RAW = 4
HI = 2
BANKS = 4
assert C_OUT + KT == C_GU[0] and C_GU[0] + 2 * BT == C_DN[0] and C_DN[0] + 2 * KT == C_GU[1]
assert C_DN[1] + 2 * KT == N_CHUNKS and N_CHUNKS % RAW == 0 and N_TILES % BANKS == 0

G_PREMIX, G_POSTMIX, G_PREFFN, G_POSTFFN, G_RET, G_ML, G_PS, N_GAINS = 0, 16, 32, 48, 64, 70, 76, 80


def tables():
    f = np.float32
    half = RD // 2
    inv = f(10000.0) ** (-np.arange(half, dtype=f) / f(half))
    pos = np.concatenate([np.arange(SEQ, dtype=f), np.full(BATCH_S, PAST, f)])
    ang = (pos[None, :] * inv[:, None]).astype(f)
    cos, sin = np.cos(ang.astype(np.float64)), np.sin(ang.astype(np.float64))
    c2, s2 = np.concatenate([cos, cos]), np.concatenate([sin, -sin])
    sc = RD ** -0.5
    rope = np.stack([c2, s2, c2 * sc, s2 * sc], 1).astype(f)
    lg = np.log1p(-np.exp2(-5.0 - np.arange(RH)))
    i = np.arange(CH)
    diff = i[None, :] - i[:, None]
    dec = np.where(diff[:, None, :] >= 0, np.exp(lg[None, :, None] * np.maximum(diff, 0)[:, None, :]), 0.0)
    decq = np.broadcast_to(np.exp(lg[:, None] * (i + 1.0))[None], (P, RH, CH))
    deck = np.exp(lg[None, :] * (CH - 1.0 - i)[:, None])
    ident = np.eye(P)
    ones = np.ones((P, P))
    mask = np.where(diff >= 0, 0.0, -1e30)
    sel = np.zeros((P, MH, P))
    for h in range(MH):
        sel[h, h] = 1.0
    m8 = np.zeros((P, BATCH_S))
    m8[:BATCH_S] = np.eye(BATCH_S)
    invc = np.zeros((P, PG, 16))
    for g in range(PG):
        invc[:, g] = 1.0 / np.minimum(np.arange(16) + 1.0, 2.0 ** (g + 1))
    parts = [rope, dec, decq, deck, ident, ones, mask, sel, m8, invc]
    flat = np.concatenate([np.ascontiguousarray(a.astype(f)).reshape(P, -1) for a in parts], 1)
    gamma = [float(np.exp(v)) for v in lg]
    gchunk = [float(np.exp(v * CH)) for v in lg]
    return np.ascontiguousarray(flat), gamma, gchunk


TABLE_SIZES = [4 * TOK, RH * CH, RH * CH, RH, P, P, P, MH * P, BATCH_S, PG * 16]


class Chain:

    def __init__(self, eng, sem, layer, per_layer):
        self.eng, self.sem, self.base, self.k, self.per_layer = eng, sem, layer * per_layer, 0, per_layer

    def __call__(self, ins):
        ins.then_inc(self.sem, 1)
        self.k += 1
        self.eng.wait_ge(self.sem, self.base + self.k)
        return ins

    def close(self):
        assert self.k == self.per_layer, (self.sem, self.k, self.per_layer)


def build(nc, a, gamma, gchunk):
    with ExitStack() as ctx:
        used = [0]
        arena = ctx.enter_context(nc.sbuf_tensor("arena", [P, 212800 // 4], F32))
        base0 = nc.sbuf_base() if callable(nc.sbuf_base) else nc.sbuf_base
        start = base0 - 212800

        def place(name, shape, dt, at=None):
            n = 4
            for s in shape[1:]:
                n *= s
            if at is None:
                at = used[0]
                used[0] += (n + 31) // 32 * 32
                assert used[0] <= 212800, (name, used[0])
            t = nc.alloc_sbuf_tensor_at(name, shape, dt, offset=start + at)
            return t, at

        def psum(name):
            return ctx.enter_context(nc.psum_tensor(name, [P, 512], F32))

        def sem(name):
            return ctx.enter_context(nc.semaphore(name))

        x, _ = place("x", [P, KT, TOK], F32)
        ahi, _ = place("ahi", [P, KT, TOK], F32R)
        alo, _ = place("alo", [P, KT, TOK], F32R)
        raw, at_raw = place("raw", [P, RAW, CHUNK], F32)
        wlo, _ = place("wlo", [P, RAW, CHUNK], F32R, at_raw)
        whi, _ = place("whi", [P, HI, CHUNK], F32R)
        proj, at_proj = place("proj", [P, NPROJ, TOK], F32)
        hhi, _ = place("hhi", [P, BT, TOK], F32R, at_proj)
        hlo, _ = place("hlo", [P, BT, TOK], F32R, at_proj + 4 * BT * TOK)
        table, _ = place("table", [P, sum(TABLE_SIZES)], F32)
        gains, _ = place("gains", [P, DEPTH, N_GAINS], F32)
        wpool, _ = place("wpool", [P, PG, P], F32)
        gbias, _ = place("gbias", [P, DEPTH, 2], F32)
        sq, _ = place("sq", [P, 4, TOK], F32)
        ssq, _ = place("ssq", [P, TOK], F32)
        rms, _ = place("rms", [P, TOK], F32)
        rstd, _ = place("rstd", [P, TOK], F32)
        epsc, _ = place("epsc", [P, 1], F32)
        marks, _ = place("marks", [P, 8], F32)
        zero, _ = place("zero", [P, TOK], F32)
        WORK = (212800 - used[0]) // 4 - 8
        work, at_work = place("work", [P, WORK], F32)
        acc = work[:, 0:KT * TOK].rearrange("p (k t) -> p k t", k=KT)
        wofs = [KT * TOK]

        def tmp(*shape):
            n = 1
            for s in shape:
                n *= s
            v = work[:, wofs[0]:wofs[0] + n]
            wofs[0] += n
            assert wofs[0] <= WORK, (wofs[0], WORK)
            if len(shape) == 2:
                v = v.rearrange("p (a b) -> p a b", a=shape[0])
            if len(shape) == 3:
                v = v.rearrange("p (a b c) -> p a b c", a=shape[0], b=shape[1])
            return v

        ga, sg, ua, hs = tmp(2, TOK), tmp(2, TOK), tmp(2, TOK), tmp(2, TOK)
        wofs[0] = 0
        rot_a, rot_b, qrot, krot = tmp(2, TOK), tmp(2, TOK), tmp(TOK), tmp(TOK)
        qdec = tmp(CH)
        vtok, ktok = tmp(2, CH), tmp(2, CH)
        vks = tmp(2, CH)
        vdiag = tmp(BATCH_S, CH)
        S = tmp(2, BATCH_S, CH)
        S1, S2, sT = tmp(CH), tmp(2, CH), tmp(2, CH)
        r_end = wofs[0]
        wofs[0] = 0
        mvtok = tmp(2, MV * MH)
        mvs = tmp(MV * MH)
        gates = tmp(2, TOK)
        lfa, lfb, lft = tmp(TOK), tmp(TOK), tmp(TOK)
        bcum, gpre, mrun, mst = tmp(TOK), tmp(TOK), tmp(TOK), tmp(TOK)
        rows1 = tmp(2 * SEQ)
        NR2 = CH + 3 * BATCH_S
        rows2 = tmp(NR2)
        wT, en, ab, msT, kw, aq = tmp(2, CH), tmp(TOK), tmp(NR2), tmp(2, CH), tmp(2, MQK), tmp(CH)
        gcol = tmp(2, MH)
        C1, C2 = tmp(MV), tmp(2, MV)
        n1, n2, nrep, kws, kwst, nsn, qn = tmp(2), tmp(MH), tmp(P), tmp(BATCH_S), tmp(P), tmp(MH, BATCH_S), tmp(BATCH_S)
        m0s, mfin, mss = tmp(BATCH_S), tmp(2), tmp(BATCH_S)
        PW = SEQ + 16
        pa, pb = tmp(PW), tmp(PW)
        free = proj[:, T_RK:T_RK + 12, :].rearrange("p a t -> p (a t)")
        Cs = free[:, 0:BATCH_S * MV].rearrange("p (b v) -> p b v", b=BATCH_S)
        cdiag = free[:, BATCH_S * MV:2 * BATCH_S * MV].rearrange("p (b v) -> p b v", b=BATCH_S)
        pfree = proj[:, T_RG:T_RG + 6, :].rearrange("p a t -> p (a t)")
        pwin = pfree[:, 0:PG * BATCH_S * 16].rearrange("p (g b i) -> p g b i", g=PG, b=BATCH_S)
        psum_s = pfree[:, 512:512 + PG * BATCH_S].rearrange("p (g b) -> p g b", g=PG)

        o = [0]
        for n in TABLE_SIZES:
            o.append(o[-1] + n)
        view = [table[:, o[i]:o[i + 1]] for i in range(len(TABLE_SIZES))]
        rope = view[0].rearrange("p (a t) -> p a t", a=4)
        dec = view[1].rearrange("p (h t) -> p h t", h=RH)
        decq = view[2].rearrange("p (h t) -> p h t", h=RH)
        deck, ident, ones, mask = view[3:7]
        sel = view[7].rearrange("p (h m) -> p h m", h=MH)
        m8 = view[8]
        invc = view[9].rearrange("p (g i) -> p g i", g=PG)

        bank = [psum(f"bank{i}") for i in range(8)]

        raw_landed = [sem(f"raw_landed{i}") for i in range(RAW)]
        x_landed, const_landed = sem("x_landed"), sem("const_landed")
        hi_made = sem("hi_made")
        chunk_split = sem("chunk_split")
        chunk_used = sem("chunk_used")
        tile_evac = sem("tile_evac")
        operand_hi = sem("operand_hi")
        operand_ready = sem("operand_ready")
        x_updated = sem("x_updated")
        sq_made, sq_added = sem("sq_made"), sem("sq_added")
        ssq_summed, rms_made, rstd_made = sem("ssq_summed"), sem("rms_made"), sem("rstd_made")
        silu_made = sem("silu_made")
        hidden_made = sem("hidden_made")
        hidden_hi = sem("hidden_hi")
        hidden_ready = sem("hidden_ready")
        dve_done, act_done, pool_done = sem("dve_done"), sem("act_done"), sem("pool_done")
        ret_rotated, ret_turned, ret_scored = sem("ret_rotated"), sem("ret_turned"), sem("ret_scored")
        ret_vk, ret_vks, ret_weighted, ret_diag = sem("ret_vk"), sem("ret_vks"), sem("ret_weighted"), sem("ret_diag")
        ret_grown, ret_outer, ret_s1, ret_s2 = sem("ret_grown"), sem("ret_outer"), sem("ret_s1"), sem("ret_s2")
        ret_snew, ret_out, ret_kept = sem("ret_snew"), sem("ret_out"), sem("ret_kept")
        S_landed, S_stored = [sem("S_landed0"), sem("S_landed1")], [sem("S_stored0"), sem("S_stored1")]
        S2_stored = sem("S2_stored")
        ret_normsum, ret_rms, ret_silu, ret_mixed, ret_hi = (sem("ret_normsum"), sem("ret_rms"), sem("ret_silu"),
                                                             sem("ret_mixed"), sem("ret_hi"))
        ml_abs, ml_log, ml_rows, ml_a1, ml_gturn, ml_gcol = (sem("ml_abs"), sem("ml_log"), sem("ml_rows"),
                                                             sem("ml_a1"), sem("ml_gturn"), sem("ml_gcol"))
        ml_vturned, ml_vtok = sem("ml_vturned"), sem("ml_vtok")
        ml_spread, ml_weights, ml_scored, ml_keys, ml_kws = (sem("ml_spread"), sem("ml_weights"), sem("ml_scored"),
                                                             sem("ml_keys"), sem("ml_kws"))
        ml_kwst, ml_kwsc, ml_grown, ml_c1, ml_c2 = (sem("ml_kwst"), sem("ml_kwsc"), sem("ml_grown"), sem("ml_c1"),
                                                    sem("ml_c2"))
        ml_outer, ml_cs, ml_num, ml_h = sem("ml_outer"), sem("ml_cs"), sem("ml_num"), sem("ml_h")
        ml_sq, ml_normsum, ml_rms, ml_sig, ml_mixed, ml_hi = (sem("ml_sq"), sem("ml_normsum"), sem("ml_rms"),
                                                              sem("ml_sig"), sem("ml_mixed"), sem("ml_hi"))
        C_landed, C_stored, C2_stored, n_landed, m_landed = (sem("C_landed"), sem("C_stored"), sem("C2_stored"),
                                                             sem("n_landed"), sem("m_landed"))
        rows_stored, nm_stored = sem("rows_stored"), sem("nm_stored")
        pl_landed, pl_ready, pl_summed, pl_z, pl_y, pl_mixed, pl_hi, pl_stored = (
            sem("pl_landed"), sem("pl_ready"), sem("pl_summed"), sem("pl_z"), sem("pl_y"), sem("pl_mixed"),
            sem("pl_hi"), sem("pl_stored"))
        y_stored, wpool_landed = sem("y_stored"), sem("wpool_landed")

        passed = {}

        def apart(eng):
            eng.sem_inc(passed[eng.engine], 1)

        for engine in (nc.tensor, nc.vector, nc.gpsimd):
            passed[engine.engine] = sem(f"passed_{len(passed)}")
        block = ctx.enter_context(nc.Block())

        @block.sync
        def _(sp):
            sp.dma_start(x[:], a["xT"]).then_inc(x_landed, 16)
            with sp.Fori(0, DEPTH) as l:

                def load(n, slot, src, words):
                    sp.wait_ge(chunk_used, n + 1)
                    sp.dma_start(raw[:, slot, 0:words], src).then_inc(raw_landed[slot], 16)

                with sp.Fori(0, NPROJ // RAW) as i:
                    for j in range(RAW):
                        load(l * N_CHUNKS + C_IN + i * RAW + j, j, a["w_in"][l * NPROJ + i * RAW + j], CHUNK)
                with sp.Fori(0, KT // RAW) as i:
                    for j in range(RAW):
                        load(l * N_CHUNKS + C_OUT + i * RAW + j, j, a["w_out"][l * KT + i * RAW + j], CHUNK)
                for b in range(NBLK):
                    with sp.Fori(0, 2 * BT // RAW) as i:
                        for j in range(RAW):
                            load(l * N_CHUNKS + C_GU[b] + i * RAW + j, j,
                                 a["w_gu"][l * 2 * FT + b * 2 * BT + i * RAW + j], CHUNK)
                    with sp.Fori(0, 2 * KT // RAW) as i:
                        for j in range(RAW):
                            load(l * N_CHUNKS + C_DN[b] + i * RAW + j, j,
                                 a["w_dn"][(l * NBLK + b) * 2 * KT + i * RAW + j], HALF)
            sp.wait_ge(x_updated, DEPTH * 8 + 4)
            sp.dma_start(a["yT"], x[:]).then_inc(y_stored, 16)
            sp.wait_ge(y_stored, 16)

        @block.tensor
        def _(pe):
            pe.wait_ge(const_landed, 16 * 3)
            with pe.Fori(0, DEPTH) as l:

                def norm_sum(e):
                    pe.wait_ge(sq_added, l * 64 + e * 16 + 16 + 4)
                    pe.wait_ge(rms_made, l * 4 + e)
                    pe.matmul(bank[4][:, 0:TOK], ones, ssq[:], start=True, stop=True).then_inc(ssq_summed, 1)

                def chunk(n, slot, out, hi, lo, ks, start, stop):
                    pe.wait_ge(chunk_split, n + 1)
                    for k in range(ks):
                        w = bass.ds(k * P, P)
                        first, last = start and k == 0, stop and k == ks - 1
                        pe.matmul(out, whi[:, slot % HI, w], hi[:, k, :], start=first, stop=False)
                        pe.matmul(out, whi[:, slot % HI, w], lo[:, k, :], start=False, stop=False)
                        mm = pe.matmul(out, wlo[:, slot, w], hi[:, k, :], start=False, stop=last)
                    mm.then_inc(chunk_used, 1)

                def whole(bodies, c0, o0):
                    apart(pe)
                    with pe.Fori(0, bodies) as i:
                        for j in range(RAW):
                            pe.wait_ge(tile_evac, l * N_TILES + o0 + i * RAW + j + 1)
                            chunk(l * N_CHUNKS + c0 + i * RAW + j, j, bank[j][:, 0:TOK], ahi[:], alo[:], KT, True, True)

                def turn(out, in_, n=P):
                    return pe.matmul(out, in_, ident[0:n, 0:n], is_transpose=True, start=True, stop=True)

                norm_sum(0)
                pe.wait_ge(operand_ready, l * 3 + 1)
                whole(NPROJ // RAW, C_IN, O_IN)

                pe.wait_ge(tile_evac, l * N_TILES + NPROJ + BANKS)
                for h in range(RH):
                    r = l * RH + h
                    pe.wait_ge(ret_rotated, r + 1)
                    pe.wait_ge(ret_kept, r)
                    pe.wait_ge(ret_snew, r)
                    for c in range(2):
                        turn(bank[4][:, c * CH:(c + 1) * CH], proj[:, T_RV + h, c * CH:(c + 1) * CH])
                        turn(bank[4][:, (2 + c) * CH:(3 + c) * CH], krot[:, c * CH:(c + 1) * CH])
                    turn(bank[5][0:BATCH_S, 0:P], proj[:, T_RV + h, SEQ:TOK])
                    turn(bank[5][0:BATCH_S, P:2 * P], krot[:, SEQ:TOK]).then_inc(ret_turned, 1)
                    for c in range(2):
                        t = slice(c * CH, (c + 1) * CH)
                        mm = pe.matmul(bank[6][:, t], krot[:, t], qrot[:, t], start=True, stop=True)
                    mm.then_inc(ret_scored, 1)
                    pe.wait_ge(ret_vk, r + 1)
                    pe.wait_ge(ret_s2, r)
                    for c in range(2):
                        mm = pe.matmul(bank[7][:, c * CH:(c + 1) * CH], ktok[:, c, :], vtok[:, c, :], start=True, stop=True)
                    mm.then_inc(ret_grown, 1)
                    pe.wait_ge(ret_diag, r + 1)
                    for i in range(2):
                        mm = pe.matmul(bank[4 + i][:, 0:512], vks[0:BATCH_S, 1, :],
                                       vdiag[0:BATCH_S, 4 * i:4 * i + 4, :].rearrange("p b v -> p (b v)"),
                                       start=True, stop=True)
                    mm.then_inc(ret_outer, 1)
                    pe.wait_ge(ret_weighted, r + 1)
                    pe.wait_ge(ret_s1, r + 1)
                    pe.matmul(bank[6][:, 0:CH], vtok[:, 0, :], sT[:, 0, :], start=True, stop=True)
                    pe.matmul(bank[6][:, CH:SEQ], vtok[:, 1, :], sT[:, 1, :], start=True, stop=False)
                    pe.matmul(bank[6][:, CH:SEQ], S1, qdec, start=False, stop=True)
                    pe.wait_ge(ret_snew, r + 1)
                    for b in range(BATCH_S):
                        mm = pe.matmul(bank[6][:, SEQ + b:SEQ + b + 1], S[:, h % 2, b, :], qrot[:, SEQ + b:SEQ + b + 1],
                                       start=True, stop=True)
                    mm.then_inc(ret_out, 1)
                pe.wait_ge(ret_kept, l * RH + RH)
                for h in range(RH):
                    mm = pe.matmul(bank[h][:, 0:TOK], ones, proj[:, T_RK + h, :], start=True, stop=True)
                mm.then_inc(ret_normsum, 1)

                pe.wait_ge(ret_rms, l + 1)
                for i in range(6):
                    for c in range(2):
                        k = 2 * i + c
                        turn(bank[k // 4][:, (k % 4) * P:(k % 4 + 1) * P], proj[:, T_MV + i, c * CH:(c + 1) * CH])
                    k = i if i < 4 else i - 4
                    turned = turn(bank[3 + i // 4][0:BATCH_S, k * P:(k + 1) * P], proj[:, T_MV + i, SEQ:TOK])
                turned.then_inc(ml_vturned, 1)
                pe.wait_ge(ml_rows, l + 1)
                apart(pe)
                for c in range(2):
                    mm = turn(bank[5][:, c * MH:(c + 1) * MH], gpre[0:MH, c * CH:(c + 1) * CH], MH)
                mm.then_inc(ml_gturn, 1)
                pe.wait_ge(ml_vtok, l + 1)
                pe.wait_ge(ml_gcol, l + 1)
                pe.wait_ge(ml_a1, l + 1)
                pe.wait_ge(act_done, l * 3 + 2)
                for h in range(MH):
                    q = l * MH + h
                    pair, odd = h // 2, h % 2
                    qt, kt_ = proj[0:MQK, T_MQ + h, :], proj[0:MQK, T_MK + h, :]
                    pe.wait_ge(ml_h, q)
                    pe.matmul(bank[4][:, 0:2 * SEQ], sel[0:MH, h, :], rows1[0:MH, :], start=True, stop=False,
                              skip_group_check=True)
                    for c in range(2):
                        pe.matmul(bank[4][:, c * CH:(c + 1) * CH], ident, mask, start=False, stop=(c == 1),
                                  skip_group_check=True)
                    pe.matmul(bank[5][:, 0:NR2], sel[0:MH, h, :], rows2[0:MH, :], start=True, stop=True)\
                        .then_inc(ml_spread, 1)
                    pe.wait_ge(ml_c2, q)
                    for c in range(2):
                        turn(bank[6][:, c * MQK:(c + 1) * MQK], kt_[:, c * CH:(c + 1) * CH], MQK)
                    for c in range(2):
                        t = slice(c * CH, (c + 1) * CH)
                        mm = pe.matmul(bank[7][:, t], kt_[:, t], qt[:, t], start=True, stop=True)
                    mm.then_inc(ml_scored, 1)
                    pe.wait_ge(ml_kws, q + 1)
                    turn(bank[6][0:BATCH_S, 400:400 + MQK], kws[0:MQK, :], MQK).then_inc(ml_kwst, 1)
                    pe.wait_ge(ml_kwsc, q + 1)
                    for c in range(2):
                        pe.matmul(bank[6][0:MQK, c * MV:(c + 1) * MV], kw[:, c, :], mvtok[:, c, h * MV:(h + 1) * MV],
                                  start=True, stop=True)
                        mm = pe.matmul(bank[6][0:MQK, 400 + c:401 + c], kw[:, c, :], ones[:, 0:1], start=True, stop=True)
                    mm.then_inc(ml_grown, 1)
                    pe.wait_ge(ml_cs, q)
                    for i in range(4):
                        mm = pe.matmul(bank[i][0:MQK, 0:2 * MV], kwst[0:BATCH_S, 0:MQK],
                                       cdiag[0:BATCH_S, 2 * i:2 * i + 2, :].rearrange("p b v -> p (b v)"),
                                       start=True, stop=True)
                    mm.then_inc(ml_outer, 1)
                    pe.wait_ge(ml_c1, q + 1)
                    pe.wait_ge(ml_cs, q + 1)
                    big, small = (0, P) if not odd else (64, MV), (P, MV) if not odd else (0, 64)
                    for bk, (f0, f1), po in ((4, big, 0), (5, small, 64 * odd)):
                        rows = slice(po, po + f1 - f0)
                        v0 = h * MV
                        pe.matmul(bank[bk][rows, 0:CH], mvtok[:, 0, v0 + f0:v0 + f1], msT[:, 0, :], start=True, stop=True)
                        pe.matmul(bank[bk][rows, CH:SEQ], mvtok[:, 1, v0 + f0:v0 + f1], msT[:, 1, :], start=True, stop=False)
                        pe.matmul(bank[bk][rows, CH:SEQ], C1[0:MQK, f0:f1], aq[0:MQK, :], start=False, stop=True)
                        for b in range(BATCH_S):
                            pe.matmul(bank[bk][rows, SEQ + b:SEQ + b + 1], Cs[0:MQK, b, f0:f1], qt[:, SEQ + b:SEQ + b + 1],
                                      start=True, stop=True)
                    pe.matmul(bank[7][:, 0:CH], ones, msT[:, 0, :], start=True, stop=True)
                    pe.matmul(bank[7][:, CH:SEQ], ones, msT[:, 1, :], start=True, stop=False)
                    pe.matmul(bank[7][:, CH:SEQ], nrep[0:MQK, :], aq[0:MQK, :], start=False, stop=True)
                    pe.matmul(bank[7][:, SEQ:TOK], ones[0:MQK, :], qn[0:MQK, :], start=True, stop=True).then_inc(ml_num, 1)
                pe.wait_ge(ml_sq, l + 1)
                for h in range(MH):
                    odd, t0 = h % 2, T_MQ + 3 * (h // 2)
                    bk = bank[4 + h][:, 0:TOK]
                    if not odd:
                        pe.matmul(bk, ones, proj[:, t0, :], start=True, stop=False)
                        mm = pe.matmul(bk, ones[0:64, :], proj[0:64, t0 + 1, :], start=False, stop=True)
                    else:
                        pe.matmul(bk, ones[64:128, :], proj[64:128, t0 + 1, :], start=True, stop=False)
                        mm = pe.matmul(bk, ones, proj[:, t0 + 2, :], start=False, stop=True)
                mm.then_inc(ml_normsum, 1)

                pe.wait_ge(wpool_landed, l * 16 + 16)
                for g in range(PG):
                    pe.wait_ge(pl_z, l * PG + g + 1)
                    mm = pe.matmul(bank[g][:, 0:TOK], wpool[:, g, :], proj[:, T_PU + g, :], start=True, stop=True)
                mm.then_inc(pl_y, 1)

                pe.wait_ge(operand_ready, l * 3 + 2)
                whole(KT // RAW, C_OUT, O_OUT)
                norm_sum(1)
                norm_sum(2)
                pe.wait_ge(operand_ready, l * 3 + 3)
                for b in range(NBLK):
                    whole(2 * BT // RAW, C_GU[b], O_GU[b])
                    pe.wait_ge(hidden_ready, l * FT + (b + 1) * BT)
                    apart(pe)
                    with pe.Fori(0, KT // 4) as i:
                        for j in range(8):
                            u, half = j // 2, j % 2
                            if half == 0:
                                pe.wait_ge(tile_evac, l * N_TILES + O_DN[b] + i * 4 + u + 1)
                            hh = slice(half * HT, (half + 1) * HT)
                            chunk(l * N_CHUNKS + C_DN[b] + i * 8 + j, j % RAW, bank[u][:, 0:TOK], hhi[:, hh, :], hlo[:, hh, :],
                                  HT, half == 0, half == 1)
                norm_sum(3)

        @block.scalar
        def _(act):
            act.dma_start(table[:], a["table"]).then_inc(const_landed, 16)
            act.dma_start(gains[:], a["gains"]).then_inc(const_landed, 16)
            act.dma_start(gbias[0:MH], a["gbias"]).then_inc(const_landed, 16)
            act.wait_ge(const_landed, 16 * 3)
            act.wait_ge(x_landed, 16)
            act.wait_ge(dve_done, 2)
            with act.Fori(0, DEPTH) as l:

                def hi_part(n, slot, words):
                    act.wait_ge(raw_landed[slot], (n - slot) * 4 + 16)
                    act.wait_ge(chunk_used, n - HI + 1 + RAW)
                    act.activation(whi[:, slot % HI, 0:words], raw[:, slot, 0:words], ACT.Copy).then_inc(hi_made, 1)

                def square(e, k, src, slot):
                    act.wait_ge(sq_added, l * 64 + e * 16 + k + 1)
                    act.activation(sq[:, slot, :], src, ACT.Square).then_inc(sq_made, 1)

                def operand(m, e, gain):
                    for k in range(KT):
                        if k % 4 == 0:
                            act.wait_ge(x_updated, l * 8 + m * 4 + k // 4 + 1)
                        act.activation(ahi[:, k, :], x[:, k, :], ACT.Copy, scale=gains[:, l, gain + k:gain + k + 1])\
                            .then_inc(operand_hi, 1)
                        square(e, k, x[:, k, :], k % 4)

                def make_rms(e):
                    act.wait_ge(ssq_summed, l * 4 + e + 1)
                    act.wait_ge(rstd_made, l * 4 + e)
                    act.activation(rms[:], bank[4][:, 0:TOK], ACT.Sqrt, scale=1.0 / D_MODEL, bias=epsc[:])\
                        .then_inc(rms_made, 1)

                c0 = l * N_CHUNKS
                hi_part(c0, 0, CHUNK)
                operand(0, 0, G_PREMIX)
                make_rms(0)
                with act.Fori(0, NPROJ // RAW) as i:
                    for j in range(RAW):
                        hi_part(c0 + C_IN + i * RAW + j + 1, (j + 1) % RAW, CHUNK)

                for h in range(RH):
                    r = l * RH + h
                    act.wait_ge(ret_turned, r + 1)
                    act.activation(vtok[:], bank[4][:, 0:SEQ].rearrange("p (c f) -> p c f", c=2), ACT.Copy)
                    act.activation(ktok[:], bank[4][:, SEQ:2 * SEQ].rearrange("p (c f) -> p c f", c=2), ACT.Copy,
                                   scale=deck[:, h:h + 1]).then_inc(ret_vk, 1)
                    act.activation(vks[0:BATCH_S], bank[5][0:BATCH_S, 0:2 * P].rearrange("p (c f) -> p c f", c=2),
                                   ACT.Copy).then_inc(ret_vks, 1)
                    act.wait_ge(ret_grown, r + 1)
                    act.activation(S1, bank[7][:, 0:CH], ACT.Copy).then_inc(ret_s1, 1)
                    act.wait_ge(ret_out, r + 1)
                    act.activation(proj[:, T_RQ + h, :], bank[6][:, 0:TOK], ACT.Copy)
                    act.activation(proj[:, T_RK + h, :], bank[6][:, 0:TOK], ACT.Square).then_inc(ret_kept, 1)
                act.wait_ge(ret_normsum, l + 1)
                for h in range(RH):
                    s_ = act.activation(proj[:, T_RV + h, :], bank[h][:, 0:TOK], ACT.Sqrt, scale=1.0 / RD, bias=epsc[:])
                s_.then_inc(ret_rms, 1)
                act.activation(proj[:, T_RG:T_RG + RH, :], proj[:, T_RG:T_RG + RH, :], ACT.Silu).then_inc(ret_silu, 1)
                act.wait_ge(ret_mixed, l + 1)
                act.activation(ahi[:, X_RET:X_RET + 6, :], proj[:, T_RQ:T_RQ + 6, :], ACT.Copy).then_inc(ret_hi, 1)

                act.wait_ge(ml_abs, l + 1)
                act.activation(lfb[0:MH, :], lfa[0:MH, :], ACT.Exp).then_inc(act_done, 1)
                act.wait_ge(act_done, l * 3 + 1)
                act.activation(lfb[0:MH, :], lfb[0:MH, :], ACT.Ln, bias=ones[0:MH, 0:1]).then_inc(ml_log, 1)
                act.wait_ge(ml_vturned, l + 1)
                for i in range(3):
                    act.activation(mvtok[:, :, 2 * i * P:2 * (i + 1) * P].rearrange("p c (t f) -> p t c f", t=2),
                                   bank[i][:, :].rearrange("p (t c f) -> p t c f", t=2, c=2), ACT.Copy)
                act.activation(mvs[0:BATCH_S, 0:4 * P], bank[3][0:BATCH_S, :], ACT.Copy)
                act.activation(mvs[0:BATCH_S, 4 * P:6 * P], bank[4][0:BATCH_S, 0:2 * P], ACT.Copy).then_inc(ml_vtok, 1)
                act.wait_ge(ml_gturn, l + 1)
                act.activation(gcol[:], bank[5][:, 0:2 * MH].rearrange("p (c h) -> p c h", c=2), ACT.Copy)\
                    .then_inc(ml_gcol, 1)
                act.wait_ge(ml_a1, l + 1)
                act.activation(rows2[0:MH, 0:CH], rows1[0:MH, CH:SEQ], ACT.Exp, bias=mst[0:MH, CH - 1:CH])
                act.activation(rows2[0:MH, CH:NR2], lft[0:MH, 0:3 * BATCH_S], ACT.Exp).then_inc(act_done, 1)
                for h in range(MH):
                    q = l * MH + h
                    act.wait_ge(ml_spread, q + 1)
                    act.wait_ge(ml_gcol, l + 1)
                    for c in range(2):
                        act.activation(wT[:, c, :], bank[4][:, c * CH:(c + 1) * CH], ACT.Exp, bias=gcol[:, c, h:h + 1])
                    act.activation(en[:, 0:SEQ], bank[4][:, SEQ:2 * SEQ], ACT.Exp)
                    act.activation(en[:, SEQ:TOK], bank[5][:, NR2 - BATCH_S:NR2], ACT.Copy)
                    act.activation(ab[:], bank[5][:, 0:NR2], ACT.Copy).then_inc(ml_weights, 1)
                    act.wait_ge(ml_grown, q + 1)
                    act.activation(n1[0:MQK, 0:1], bank[6][0:MQK, 400:401], ACT.Copy)
                    act.activation(C1[0:MQK, :], bank[6][0:MQK, 0:MV], ACT.Copy).then_inc(ml_c1, 1)
                act.wait_ge(ml_h, l * MH + MH)
                act.activation(proj[:, T_MQ:T_MQ + 6, :], proj[:, T_MV:T_MV + 6, :], ACT.Square).then_inc(ml_sq, 1)
                act.wait_ge(ml_normsum, l + 1)
                for h in range(MH):
                    s_ = act.activation(proj[:, T_RV + h, :], bank[4 + h][:, 0:TOK], ACT.Sqrt, scale=1.0 / MV, bias=epsc[:])
                s_.then_inc(ml_rms, 1)
                act.activation(proj[:, T_MO:T_MO + 6, :], proj[:, T_MO:T_MO + 6, :], ACT.Sigmoid).then_inc(ml_sig, 1)
                act.wait_ge(ml_mixed, l + 1)
                act.activation(ahi[:, X_ML:X_ML + 6, :], proj[:, T_MV:T_MV + 6, :], ACT.Copy).then_inc(ml_hi, 1)

                act.wait_ge(pl_y, l + 1)
                for g in range(PG):
                    s_ = act.activation(proj[:, T_PU + g, :], bank[g][:, 0:TOK], ACT.Copy,
                                        scale=gains[:, l, G_PS + g:G_PS + g + 1])
                s_.then_inc(act_done, 1)
                act.wait_ge(act_done, l * 3 + 3)
                act.activation(ahi[:, X_POOL:X_POOL + 4, :], proj[:, T_PU:T_PU + 4, :], ACT.Copy).then_inc(pl_hi, 1)

                with act.Fori(0, KT // RAW) as i:
                    for j in range(RAW):
                        hi_part(c0 + C_OUT + i * RAW + j + 1, (j + 1) % RAW, CHUNK)
                        act.wait_ge(tile_evac, l * N_TILES + O_OUT + i * RAW + j + 1 + BANKS)
                        square(1, i * RAW + j, acc[:, i * RAW + j, :], j)
                make_rms(1)
                operand(1, 2, G_PREFFN)
                make_rms(2)

                for b in range(NBLK):

                    def gate_up(i, words_last):
                        for j in range(RAW):
                            u = j // 2
                            words = words_last if j == RAW - 1 else CHUNK
                            hi_part(c0 + C_GU[b] + i * RAW + j + 1, (j + 1) % RAW, words)
                            f = l * FT + b * BT + i * 2 + u
                            if j % 2 == 0:
                                act.wait_ge(tile_evac, l * N_TILES + O_GU[b] + i * RAW + j + 1 + BANKS)
                                act.wait_ge(hidden_made, f + 1)
                                act.activation(sg[:, u, :], ga[:, u, :], ACT.Silu).then_inc(silu_made, 1)
                            else:
                                act.wait_ge(hidden_made, f + 1 + 2)
                                act.activation(hhi[:, i * 2 + u, :], hs[:, u, :], ACT.Copy).then_inc(hidden_hi, 1)

                    with act.Fori(0, 2 * BT // RAW - 1) as i:
                        gate_up(i, CHUNK)
                    gate_up(2 * BT // RAW - 1, HALF)

                    def down(i, words_last):
                        for j in range(8):
                            words = words_last if j == 7 else HALF
                            if words:
                                hi_part(c0 + C_DN[b] + i * 8 + j + 1, (j + 1) % RAW, words)
                            if j % 2 and b == NBLK - 1:
                                act.wait_ge(tile_evac, l * N_TILES + O_DN[b] + i * 4 + j // 2 + 1 + BANKS)
                                square(3, i * 4 + j // 2, acc[:, i * 4 + j // 2, :], j // 2)

                    with act.Fori(0, KT // 4 - 1) as i:
                        down(i, HALF)
                    down(KT // 4 - 1, CHUNK if b == 0 else 0)
                make_rms(3)

        @block.vector
        def _(dve):
            dve.memset(epsc[:], EPS).then_inc(dve_done, 1)
            dve.memset(zero[:], 0.0).then_inc(dve_done, 1)
            dve.memset(marks[:, 0:1], 0.0).then_inc(chunk_used, RAW)
            dve.memset(marks[:, 1:2], 0.0).then_inc(tile_evac, BANKS)
            dve.memset(marks[:, 2:3], 0.0).then_inc(x_updated, 4)
            dve.memset(marks[:, 3:4], 0.0).then_inc(silu_made, 2)
            dve.memset(marks[:, 4:5], 0.0).then_inc(hidden_made, 2)
            dve.memset(marks[:, 5:6], 0.0).then_inc(hidden_hi, 2)
            dve.memset(marks[:, 6:7], 0.0).then_inc(sq_added, 4)
            dve.wait_ge(const_landed, 16 * 3)
            dve.wait_ge(x_landed, 16)
            with dve.Fori(0, DEPTH) as l:
                ch = Chain(dve, dve_done, l, DVE_STEPS)
                ch.base = ch.base + 2
                c0, t0 = l * N_CHUNKS, l * N_TILES

                def lo_part(n, slot, words):
                    dve.wait_ge(hi_made, n + 1)
                    w = slice(0, words)
                    dve.tensor_tensor(wlo[:, slot, w], raw[:, slot, w], whi[:, slot % HI, w].bitcast(F32), ALU.subtract)\
                        .then_inc(chunk_split, 1)

                def operand(gain, ev):
                    for k in range(KT):
                        dve.wait_ge(operand_hi, l * 2 * KT + ev * KT + k + 1)
                        ins = dve.scalar_tensor_tensor(out=alo[:, k, :], in0=x[:, k, :], scalar=gains[:, l, gain + k:gain + k + 1],
                                                       in1=ahi[:, k, :].bitcast(F32), op0=ALU.mult, op1=ALU.subtract)
                    ins.then_inc(operand_ready, 1)

                def make_rstd(e):
                    dve.wait_ge(rms_made, l * 4 + e + 1)
                    dve.reciprocal(rstd[:], rms[:]).then_inc(rstd_made, 1)
                    dve.wait_ge(rstd_made, l * 4 + e + 1)

                def update(gain):
                    for k in range(KT):
                        ins = dve.scalar_tensor_tensor(out=acc[:, k, :], in0=acc[:, k, :], scalar=gains[:, l, gain + k:gain + k + 1],
                                                       in1=rstd[:], op0=ALU.mult, op1=ALU.mult)
                    ch(ins)
                    for k in range(0, KT, 4):
                        dve.tensor_tensor(x[:, k:k + 4, :], x[:, k:k + 4, :], acc[:, k:k + 4, :], ALU.add)\
                            .then_inc(x_updated, 1)

                lo_part(c0, 0, CHUNK)
                operand(G_PREMIX, 0)
                make_rstd(0)
                apart(dve)
                with dve.Fori(0, NPROJ // RAW) as i:
                    for j in range(RAW):
                        lo_part(c0 + C_IN + i * RAW + j + 1, (j + 1) % RAW, CHUNK)
                        dve.wait_ge(chunk_used, c0 + C_IN + i * RAW + j + 1 + RAW)
                        dve.tensor_tensor(proj[:, i * RAW + j, :], bank[j][:, 0:TOK], rstd[:], ALU.mult).then_inc(tile_evac, 1)
                dve.wait_ge(tile_evac, t0 + NPROJ + BANKS)

                for h in range(RH):
                    r = l * RH + h
                    dve.wait_ge(ret_out, r)
                    for src, rt, tb in ((T_RQ + h, rot_a, 0), (T_RK + h, rot_b, 2)):
                        dve.tensor_tensor(rt[:, 0, :], proj[:, src, :], rope[:, tb, :], ALU.mult)
                        dve.tensor_tensor(rt[64:128, 1, :], proj[0:64, src, :], rope[0:64, tb + 1, :], ALU.mult)
                        ins = dve.tensor_tensor(rt[0:64, 1, :], proj[64:128, src, :], rope[64:128, tb + 1, :], ALU.mult)
                    ch(ins)
                    dve.tensor_tensor(krot[:], rot_b[:, 0, :], rot_b[:, 1, :], ALU.add)
                    dve.tensor_tensor(qrot[:], rot_a[:, 0, :], rot_a[:, 1, :], ALU.add).then_inc(ret_rotated, 1)
                    dve.wait_ge(ret_rotated, r + 1)
                    dve.tensor_tensor(qdec, qrot[:, CH:SEQ], decq[:, h, :], ALU.mult)
                    dve.wait_ge(ret_scored, r + 1)
                    dve.tensor_tensor(sT[:], bank[6][:, 0:SEQ].rearrange("p (c t) -> p c t", c=2),
                                      dec[:, h:h + 1, :].broadcast_to([P, 2, CH]), ALU.mult).then_inc(ret_weighted, 1)
                    dve.wait_ge(ret_vks, r + 1)
                    B8 = BATCH_S
                    dve.tensor_tensor(vdiag[0:B8], vks[0:B8, 0:1, :].broadcast_to([B8, B8, P]),
                                      m8[0:B8].rearrange("p (b o) -> p b o", o=1).broadcast_to([B8, B8, P]), ALU.mult)\
                        .then_inc(ret_diag, 1)
                    dve.wait_ge(ret_s1, r + 1)
                    dve.wait_ge(S2_stored, r * 16)
                    dve.scalar_tensor_tensor(out=S2[:, 0, :], in0=S1, scalar=gchunk[h], in1=bank[7][:, CH:SEQ],
                                             op0=ALU.mult, op1=ALU.add).then_inc(ret_s2, 1)
                    dve.wait_ge(ret_outer, r + 1)
                    dve.wait_ge(S_landed[h % 2], (l * 3 + h // 2) * 16 + 16)
                    for i in range(2):
                        sl = S[:, h % 2, 4 * i:4 * i + 4, :].rearrange("p b v -> p (b v)")
                        ins = dve.scalar_tensor_tensor(out=sl, in0=sl, scalar=gamma[h], in1=bank[4 + i][:, 0:512],
                                                       op0=ALU.mult, op1=ALU.add)
                    ins.then_inc(ret_snew, 1)
                dve.wait_ge(ret_rms, l + 1)
                flat = lambda t, n: proj[:, t:t + n, :].rearrange("p a t -> p (a t)")
                ch(dve.reciprocal(flat(T_RV, RH), flat(T_RV, RH)))
                for h in range(RH):
                    ins = dve.scalar_tensor_tensor(out=proj[:, T_RQ + h, :], in0=proj[:, T_RQ + h, :],
                                                   scalar=gains[:, l, G_RET + h:G_RET + h + 1], in1=proj[:, T_RV + h, :],
                                                   op0=ALU.mult, op1=ALU.mult)
                ch(ins)
                dve.wait_ge(ret_silu, l + 1)
                dve.tensor_tensor(flat(T_RQ, RH), flat(T_RQ, RH), flat(T_RG, RH), ALU.mult).then_inc(ret_mixed, 1)
                dve.wait_ge(ret_mixed, l + 1)
                dve.wait_ge(ret_hi, l + 1)
                dve.tensor_tensor(alo[:, X_RET:X_RET + 6, :], proj[:, T_RQ:T_RQ + 6, :],
                                  ahi[:, X_RET:X_RET + 6, :].bitcast(F32), ALU.subtract)

                H4 = slice(0, MH)
                for s in range(2):
                    dve.wait_ge(S_stored[s], (l * 3 + 3) * 16)
                dve.wait_ge(S2_stored, (l * RH + RH) * 16)
                dve.wait_ge(rows_stored, l * 32)
                dve.tensor_copy(gates[H4, 0, :], proj[MQK:MQK + MH, T_MQ, :])
                ch(dve.tensor_copy(gates[H4, 1, :], proj[MQK:MQK + MH, T_MQ + 1, :]))
                dve.tensor_scalar(gates[H4, 0, :], gates[H4, 0, :], gbias[H4, l, 0:1], None, ALU.add)
                ch(dve.tensor_scalar(gates[H4, 1, :], gates[H4, 1, :], gbias[H4, l, 1:2], None, ALU.add))
                dve.scalar_tensor_tensor(out=lfa[H4], in0=gates[H4, 1, :], scalar=-1.0, in1=gates[H4, 1, :],
                                         op0=ALU.mult, op1=ALU.min).then_inc(ml_abs, 1)
                dve.wait_ge(ml_log, l + 1)
                ch(dve.scalar_tensor_tensor(out=lfa[H4], in0=gates[H4, 1, :], scalar=0.0, in1=lfb[H4],
                                            op0=ALU.min, op1=ALU.subtract))
                for c in range(2):
                    t = slice(c * CH, (c + 1) * CH)
                    ins = dve.tensor_tensor_scan(bcum[H4, t], ones[H4, 0:CH], lfa[H4, t], 0.0, ALU.mult, ALU.add)
                ch(ins)
                dve.tensor_tensor(gpre[H4, 0:SEQ], gates[H4, 0, 0:SEQ], bcum[H4, 0:SEQ], ALU.subtract).then_inc(ml_rows, 1)
                dve.wait_ge(ml_rows, l + 1)
                ch(dve.tensor_tensor_scan(mrun[H4, 0:CH], zero[H4, 0:CH], gpre[H4, 0:CH], 0.0, ALU.add, ALU.max))
                ch(dve.tensor_tensor(mst[H4, 0:CH], bcum[H4, 0:CH], mrun[H4, 0:CH], ALU.add))
                ch(dve.tensor_tensor_scan(mrun[H4, CH:SEQ], zero[H4, 0:CH], gpre[H4, CH:SEQ], mst[H4, CH - 1:CH],
                                          ALU.add, ALU.max))
                ch(dve.tensor_tensor(mst[H4, CH:SEQ], bcum[H4, CH:SEQ], mrun[H4, CH:SEQ], ALU.add))
                dve.tensor_copy(mfin[H4, 0:1], mst[H4, SEQ - 1:SEQ])
                dve.tensor_scalar(rows1[H4, 0:SEQ], mrun[H4, 0:SEQ], -1.0, None, ALU.mult)
                dve.tensor_scalar(rows1[H4, SEQ:2 * SEQ], mst[H4, 0:SEQ], -1.0, None, ALU.mult)
                sm = slice(SEQ, TOK)
                dve.wait_ge(m_landed, l * 16 + 16)
                ch(dve.tensor_tensor(bcum[H4, sm], lfa[H4, sm], m0s[H4], ALU.add))
                ch(dve.tensor_tensor(mss[H4], bcum[H4, sm], gates[H4, 0, sm], ALU.max))
                dve.tensor_tensor(lft[H4, 0:8], bcum[H4, sm], mss[H4], ALU.subtract)
                dve.tensor_tensor(lft[H4, 8:16], gates[H4, 0, sm], mss[H4], ALU.subtract)
                dve.tensor_scalar(proj[0:MQK, T_MK:T_MK + MH, :].rearrange("p a t -> p (a t)"),
                                  proj[0:MQK, T_MK:T_MK + MH, :].rearrange("p a t -> p (a t)"), MQK ** -0.5, None, ALU.mult)
                dve.tensor_scalar(lft[H4, 16:24], mss[H4], -1.0, None, ALU.mult).then_inc(ml_a1, 1)
                for h in range(MH):
                    q = l * MH + h
                    pair, odd = h // 2, h % 2
                    Q, B8 = slice(0, MQK), BATCH_S
                    dve.wait_ge(ml_weights, q + 1)
                    dve.wait_ge(ml_scored, q + 1)
                    dve.tensor_tensor(msT[:], bank[7][:, 0:SEQ].rearrange("p (c t) -> p c t", c=2), wT[:], ALU.mult)
                    for c in range(2):
                        dve.tensor_scalar(kw[:, c, :], bank[6][:, c * MQK:(c + 1) * MQK], wT[:, c, CH - 1:CH], None, ALU.mult)
                    dve.tensor_tensor(aq[Q], proj[Q, T_MQ + h, CH:SEQ], ab[Q, 0:CH], ALU.mult)
                    dve.tensor_tensor(kws[Q], proj[Q, T_MK + h, SEQ:TOK], ab[Q, CH + 8:CH + 16], ALU.mult).then_inc(ml_kws, 1)
                    dve.wait_ge(ml_kws, q + 1)
                    dve.wait_ge(n_landed, l * 16 + 16)
                    ch(dve.tensor_tensor(nsn[Q, h, :], nsn[Q, h, :], ab[Q, CH:CH + 8], ALU.mult))
                    ch(dve.tensor_tensor(nsn[Q, h, :], nsn[Q, h, :], kws[Q], ALU.add))
                    dve.tensor_tensor(qn[Q], nsn[Q, h, :], proj[Q, T_MQ + h, SEQ:TOK], ALU.mult)
                    dve.tensor_tensor(cdiag[0:B8], mvs[0:B8, h * MV:(h + 1) * MV].rearrange("p (o v) -> p o v", o=1)
                                      .broadcast_to([B8, B8, MV]),
                                      m8[0:B8].rearrange("p (b o) -> p b o", o=1).broadcast_to([B8, B8, MV]), ALU.mult)
                    dve.wait_ge(ml_kwst, q + 1)
                    dve.tensor_copy(kwst[0:B8, 0:MQK], bank[6][0:B8, 400:400 + MQK]).then_inc(ml_kwsc, 1)
                    dve.wait_ge(C_landed, q * 16 + 16)
                    ch(dve.tensor_tensor(Cs[Q], Cs[Q], ab[Q, CH:CH + 8].rearrange("p (b o) -> p b o", o=1)
                                         .broadcast_to([MQK, B8, MV]), ALU.mult))
                    dve.wait_ge(ml_c1, q + 1)
                    dve.wait_ge(C2_stored, q * 16)
                    dve.tensor_scalar(nrep[Q], ones[Q], n1[Q, 0:1], None, ALU.mult)
                    dve.scalar_tensor_tensor(out=n2[Q, h:h + 1], in0=n1[Q, 0:1], scalar=ab[Q, CH - 1:CH],
                                             in1=bank[6][Q, 401:402], op0=ALU.mult, op1=ALU.add)
                    dve.scalar_tensor_tensor(out=C2[Q, 0, :], in0=C1[Q], scalar=ab[Q, CH - 1:CH],
                                             in1=bank[6][Q, MV:2 * MV], op0=ALU.mult, op1=ALU.add).then_inc(ml_c2, 1)
                    dve.wait_ge(ml_outer, q + 1)
                    for i in range(4):
                        v = Cs[Q, 2 * i:2 * i + 2, :].rearrange("p b v -> p (b v)")
                        ins = dve.tensor_tensor(v, v, bank[i][Q, 0:2 * MV], ALU.add)
                    ins.then_inc(ml_cs, 1)
                    dve.wait_ge(ml_num, q + 1)
                    ch(dve.tensor_tensor(en[:], bank[7][:, 0:TOK], en[:], ALU.max))
                    ch(dve.scalar_tensor_tensor(out=en[:], in0=bank[7][:, 0:TOK], scalar=-1.0, in1=en[:],
                                                op0=ALU.mult, op1=ALU.max))
                    ch(dve.reciprocal(en[:], en[:]))
                    bigt, rows = T_MV + 3 * pair + 2 * odd, slice(64 * odd, 64 * odd + 64)
                    dve.tensor_tensor(proj[:, bigt, :], bank[4][:, 0:TOK], en[:], ALU.mult)
                    dve.tensor_tensor(proj[rows, T_MV + 3 * pair + 1, :], bank[5][rows, 0:TOK], en[rows, :], ALU.mult)\
                        .then_inc(ml_h, 1)
                dve.wait_ge(ml_rms, l + 1)
                ch(dve.reciprocal(flat(T_RV, MH), flat(T_RV, MH)))
                for h in range(MH):
                    pair, odd = h // 2, h % 2
                    for t, rows in ((3 * pair + 2 * odd, slice(0, P)), (3 * pair + 1, slice(64 * odd, 64 * odd + 64))):
                        ins = dve.scalar_tensor_tensor(out=proj[rows, T_MV + t, :], in0=proj[rows, T_MV + t, :],
                                                       scalar=gains[rows, l, G_ML + t:G_ML + t + 1],
                                                       in1=proj[rows, T_RV + h, :], op0=ALU.mult, op1=ALU.mult)
                ch(ins)
                dve.wait_ge(ml_sig, l + 1)
                dve.tensor_tensor(flat(T_MV, 6), flat(T_MV, 6), flat(T_MO, 6), ALU.mult).then_inc(ml_mixed, 1)
                dve.wait_ge(ml_mixed, l + 1)
                dve.wait_ge(ml_hi, l + 1)
                dve.tensor_tensor(alo[:, X_ML:X_ML + 6, :], proj[:, T_MV:T_MV + 6, :],
                                  ahi[:, X_ML:X_ML + 6, :].bitcast(F32), ALU.subtract)

                for g in range(PG):
                    win = 2 << g
                    u = proj[:, T_PU + g, :]
                    dve.wait_ge(pl_landed, l * 16 + 16)
                    ch(dve.tensor_copy(pwin[:, g, :, 15], u[:, SEQ:TOK]))
                    ch(dve.tensor_reduce(psum_s[:, g, :], pwin[:, g, :, 16 - win:16], AX.X, ALU.add))
                    dve.memset(pa[:, 0:16], 0.0)
                    dve.memset(pb[:, 0:16], 0.0)
                    ch(dve.tensor_copy(pa[:, 16:PW], u[:, 0:SEQ]))
                    src, dst = pa, pb
                    for s in range(g + 1):
                        ch(dve.tensor_tensor(dst[:, 16:PW], src[:, 16:PW], src[:, 16 - (1 << s):PW - (1 << s)], ALU.add))
                        src, dst = dst, src
                    ch(dve.tensor_tensor(dst[:, 0:16], src[:, 16:32], invc[:, g, :], ALU.mult))
                    dve.wait_ge(pl_stored, l * 32 + 16)
                    dve.scalar_tensor_tensor(out=u[:, 16:SEQ], in0=src[:, 32:PW], scalar=1.0 / win, in1=u[:, 16:SEQ],
                                             op0=ALU.mult, op1=ALU.subtract)
                    dve.tensor_tensor(u[:, 0:16], dst[:, 0:16], u[:, 0:16], ALU.subtract)
                    dve.scalar_tensor_tensor(out=u[:, SEQ:TOK], in0=psum_s[:, g, :], scalar=1.0 / win, in1=u[:, SEQ:TOK],
                                             op0=ALU.mult, op1=ALU.subtract).then_inc(pl_z, 1)
                dve.memset(marks[:, 7:8], 0.0).then_inc(pl_ready, 1)
                dve.wait_ge(pl_hi, l + 1)
                dve.tensor_tensor(alo[:, X_POOL:X_POOL + 4, :], proj[:, T_PU:T_PU + 4, :],
                                  ahi[:, X_POOL:X_POOL + 4, :].bitcast(F32), ALU.subtract).then_inc(operand_ready, 1)

                dve.wait_ge(nm_stored, l * 32 + 32)
                dve.wait_ge(rows_stored, l * 32 + 32)
                dve.wait_ge(C2_stored, (l * MH + MH) * 16)
                dve.wait_ge(S2_stored, (l * RH + RH) * 16)
                for s in range(2):
                    dve.wait_ge(S_stored[s], (l * 3 + 3) * 16)
                dve.wait_ge(C_stored, (l * MH + MH) * 16)
                dve.wait_ge(pl_stored, l * 32 + 32)
                apart(dve)
                with dve.Fori(0, KT // RAW) as i:
                    for j in range(RAW):
                        lo_part(c0 + C_OUT + i * RAW + j + 1, (j + 1) % RAW, CHUNK)
                        dve.wait_ge(chunk_used, c0 + C_OUT + i * RAW + j + 1 + RAW)
                        dve.tensor_copy(acc[:, i * RAW + j, :], bank[j][:, 0:TOK]).then_inc(tile_evac, 1)
                make_rstd(1)
                dve.wait_ge(tile_evac, t0 + O_OUT + KT + BANKS)
                update(G_POSTMIX)
                operand(G_PREFFN, 1)
                make_rstd(2)

                for b in range(NBLK):

                    def gate_up(i, words_last):
                        for j in range(RAW):
                            u = j // 2
                            lo_part(c0 + C_GU[b] + i * RAW + j + 1, (j + 1) % RAW, words_last if j == RAW - 1 else CHUNK)
                            dve.wait_ge(chunk_used, c0 + C_GU[b] + i * RAW + j + 1 + RAW)
                            f = l * FT + b * BT + i * 2 + u
                            t = t0 + O_GU[b] + i * RAW + j
                            if j % 2 == 0:
                                dve.wait_ge(silu_made, f + 1)
                                dve.tensor_tensor(ga[:, u, :], bank[j][:, 0:TOK], rstd[:], ALU.mult).then_inc(tile_evac, 1)
                            else:
                                dve.tensor_tensor(ua[:, u, :], bank[j][:, 0:TOK], rstd[:], ALU.mult).then_inc(tile_evac, 1)
                                dve.wait_ge(tile_evac, t + 1 + BANKS)
                                dve.wait_ge(silu_made, f + 1 + 2)
                                dve.wait_ge(hidden_hi, f + 1)
                                dve.tensor_tensor(hs[:, u, :], ua[:, u, :], sg[:, u, :], ALU.mult).then_inc(hidden_made, 1)
                                dve.wait_ge(hidden_hi, f + 1 + 2)
                                dve.wait_ge(hidden_made, f + 1 + 2)
                                dve.tensor_tensor(hlo[:, i * 2 + u, :], hs[:, u, :], hhi[:, i * 2 + u, :].bitcast(F32),
                                                  ALU.subtract).then_inc(hidden_ready, 1)

                    apart(dve)
                    with dve.Fori(0, 2 * BT // RAW - 1) as i:
                        gate_up(i, CHUNK)
                    gate_up(2 * BT // RAW - 1, HALF)

                    def down(i, words_last):
                        for j in range(8):
                            words = words_last if j == 7 else HALF
                            if words:
                                lo_part(c0 + C_DN[b] + i * 8 + j + 1, (j + 1) % RAW, words)
                            if j % 2:
                                o_, u = i * 4 + j // 2, j // 2
                                dve.wait_ge(chunk_used, c0 + C_DN[b] + i * 8 + j + 1 + RAW)
                                if b == 0:
                                    ins = dve.tensor_copy(acc[:, o_, :], bank[u][:, 0:TOK])
                                else:
                                    ins = dve.tensor_tensor(acc[:, o_, :], bank[u][:, 0:TOK], acc[:, o_, :], ALU.add)
                                ins.then_inc(tile_evac, 1)

                    apart(dve)
                    with dve.Fori(0, KT // 4 - 1) as i:
                        down(i, HALF)
                    down(KT // 4 - 1, CHUNK if b == 0 else 0)
                    dve.wait_ge(tile_evac, t0 + O_DN[b] + KT + BANKS)
                make_rstd(3)
                update(G_POSTFFN)
                ch.close()

        @block.gpsimd
        def _(pool):
            pool.wait_ge(dve_done, 2)
            with pool.Fori(0, DEPTH) as l:

                def add_square(e, k, slot, first):
                    n = l * 64 + e * 16 + k
                    pool.wait_ge(sq_made, n + 1)
                    pool.wait_ge(sq_added, n + 4)
                    pool.tensor_tensor(ssq[:], sq[:, slot, :], zero[:] if first else ssq[:], ALU.add).then_inc(sq_added, 1)

                def all_squares(e):
                    pool.wait_ge(ssq_summed, l * 4 + e)
                    for k in range(KT):
                        add_square(e, k, k % 4, k == 0)

                def looped_squares(e):
                    pool.wait_ge(ssq_summed, l * 4 + e)
                    for j in range(4):
                        add_square(e, j, j, j == 0)
                    with pool.Fori(1, KT // 4) as i:
                        for j in range(4):
                            add_square(e, i * 4 + j, j, False)

                def load_S(h):
                    pool.wait_ge(S_stored[h % 2], (l * 3 + h // 2) * 16)
                    if h >= 2:
                        pool.wait_ge(ret_out, l * RH + h - 1)
                    apart(pool)
                    pool.dma_start(S[:, h % 2, :, :], a["s_ret"][l * RH + h]).then_inc(S_landed[h % 2], 16)

                pool.wait_ge(pl_y, l)
                apart(pool)
                pool.dma_start(wpool[:], a["w_pool"][l]).then_inc(wpool_landed, 16)
                all_squares(0)
                pool.wait_ge(x_updated, l * 8 + 4)
                load_S(0)
                load_S(1)
                pool.wait_ge(tile_evac, l * N_TILES + NPROJ + BANKS)
                apart(pool)
                pool.dma_start(a["pool_p"][l], proj[:, T_PU:T_PU + PG, SEQ - PBUF:SEQ]).then_inc(pl_stored, 16)
                for h in range(RH):
                    r = l * RH + h
                    pool.wait_ge(ret_s2, r + 1)
                    apart(pool)
                    pool.dma_start(a["ret_p"][r], S2[:, 0, :]).then_inc(S2_stored, 16)
                    pool.wait_ge(ret_snew, r + 1)
                    apart(pool)
                    pool.dma_start(a["ret_s"][r], S[:, h % 2, :, :]).then_inc(S_stored[h % 2], 16)
                    if h + 2 < RH:
                        load_S(h + 2)
                pool.wait_ge(S2_stored, (l * RH + RH) * 16)
                for s in range(2):
                    pool.wait_ge(S_stored[s], (l * 3 + 3) * 16)
                pool.wait_ge(ret_mixed, l + 1)
                apart(pool)
                pool.dma_start(m0s[0:MH], a["s_m"][l]).then_inc(m_landed, 16)
                apart(pool)
                pool.dma_start(nsn[0:MQK], a["s_n"][l]).then_inc(n_landed, 16)
                apart(pool)
                pool.dma_start(pwin[:, :, :, 0:PBUF], a["s_pool"][l]).then_inc(pl_landed, 16)
                for h in range(MH):
                    q = l * MH + h
                    pool.wait_ge(C_stored, q * 16)
                    apart(pool)
                    pool.dma_start(Cs[0:MQK], a["s_c"][q]).then_inc(C_landed, 16)
                    if h == 0:
                        pool.wait_ge(ml_a1, l + 1)
                        apart(pool)
                        pool.dma_start(a["m_p"][l], mfin[0:MH, 0:1]).then_inc(rows_stored, 16)
                        apart(pool)
                        pool.dma_start(a["m_s"][l], mss[0:MH]).then_inc(rows_stored, 16)
                    pool.wait_ge(ml_c2, q + 1)
                    apart(pool)
                    pool.dma_start(a["c_p"][q], C2[0:MQK, 0, :]).then_inc(C2_stored, 16)
                    pool.wait_ge(ml_cs, q + 1)
                    pool.wait_ge(ml_num, q + 1)
                    apart(pool)
                    pool.dma_start(a["c_s"][q], Cs[0:MQK]).then_inc(C_stored, 16)
                apart(pool)
                pool.dma_start(a["n_p"][l], n2[0:MQK]).then_inc(nm_stored, 16)
                apart(pool)
                pool.dma_start(a["n_s"][l], nsn[0:MQK]).then_inc(nm_stored, 16)
                pool.wait_ge(pl_ready, l + 1)
                apart(pool)
                pool.dma_start(a["pool_s"][l], pwin[:]).then_inc(pl_stored, 16)

                looped_squares(1)
                all_squares(2)
                looped_squares(3)
            pool.wait_ge(rows_stored, DEPTH * 32)
            pool.wait_ge(nm_stored, DEPTH * 32)
            pool.wait_ge(pl_stored, DEPTH * 32)
            pool.wait_ge(S2_stored, DEPTH * RH * 16)
            pool.wait_ge(C2_stored, DEPTH * MH * 16)
            pool.wait_ge(C_stored, DEPTH * MH * 16)
            for s in range(2):
                pool.wait_ge(S_stored[s], DEPTH * RH // 2 * 16)


DVE_STEPS = 72


def kernel(x_prompt, x_sample, state_ret, state_mlstm_c, state_mlstm_n, state_mlstm_m, state_pool,
           w_in, w_out, g_ret_norm, g_mlstm_norm, b_mlstm_i, b_mlstm_f, w_pool, pool_scale,
           g_pre_mix, g_post_mix, g_pre_ffn, g_post_ffn, w_ffn_gate, w_ffn_up, w_ffn_down):
    import concourse.bacc as bacc
    from concourse.bass_utils import run_bass_kernel_spmd

    c = np.ascontiguousarray
    L = DEPTH

    def tiles(w):
        w = np.asarray(w)
        n_in, n_out = w.shape[1] // P, w.shape[2] // P
        return w.reshape(L, n_in, P, n_out, P).transpose(0, 3, 2, 1, 4)

    w_in = np.asarray(w_in)
    rw, mq = RH * RD, MH * MQK
    gate_i = 4 * rw + 2 * mq + 2 * MH * MV
    cols = [w_in[:, :, 0:4 * rw]]
    for part in range(2):
        for h in range(MH):
            s = 4 * rw + part * mq + h * MQK
            t = np.zeros((L, D_MODEL, P), w_in.dtype)
            t[:, :, 0:MQK] = w_in[:, :, s:s + MQK]
            if part == 0 and h < 2:
                t[:, :, MQK:MQK + MH] = w_in[:, :, gate_i + h * MH:gate_i + (h + 1) * MH]
            cols.append(t)
    s = 4 * rw + 2 * mq
    cols += [w_in[:, :, s:s + 2 * MH * MV], w_in[:, :, gate_i + 2 * MH:]]
    arrays = {"w_in": c(tiles(np.concatenate(cols, 2)).reshape(L * NPROJ, P, CHUNK)),
              "w_out": c(tiles(w_out).reshape(L * KT, P, CHUNK))}
    gu = np.stack([tiles(w_ffn_gate), tiles(w_ffn_up)], 2)
    arrays["w_gu"] = c(gu.reshape(L * 2 * FT, P, CHUNK))
    dn = np.asarray(w_ffn_down).reshape(L, NBLK, 2, HT, P, KT, P).transpose(0, 1, 5, 2, 4, 3, 6)
    arrays["w_dn"] = c(dn.reshape(L * NBLK * 2 * KT, P, HALF))

    toks = np.concatenate([np.asarray(x_prompt)[0], np.asarray(x_sample)[:, 0]], 0)
    arrays["xT"] = c(toks.reshape(TOK, KT, P).transpose(2, 1, 0))
    table, gamma, gchunk = tables()
    arrays["table"] = table
    by_part = lambda g: np.asarray(g).reshape(L, -1, P).transpose(2, 0, 1)
    arrays["gains"] = c(np.concatenate([by_part(g) for g in (g_pre_mix, g_post_mix, g_pre_ffn, g_post_ffn,
                                                             g_ret_norm, g_mlstm_norm, pool_scale)], 2))
    arrays["w_pool"] = c(np.asarray(w_pool).transpose(0, 2, 1, 3))
    arrays["gbias"] = c(np.stack([np.asarray(b_mlstm_i), np.asarray(b_mlstm_f)], 2).transpose(1, 0, 2))
    arrays["s_ret"] = c(np.asarray(state_ret).transpose(0, 2, 3, 1, 4).reshape(L * RH, RD, BATCH_S, RD))
    arrays["s_c"] = c(np.asarray(state_mlstm_c).transpose(0, 2, 3, 1, 4).reshape(L * MH, MQK, BATCH_S, MV))
    arrays["s_n"] = c(np.asarray(state_mlstm_n).transpose(0, 3, 2, 1))
    arrays["s_m"] = c(np.asarray(state_mlstm_m).transpose(0, 2, 1))
    arrays["s_pool"] = c(np.asarray(state_pool).reshape(L, BATCH_S, PBUF, PG, P).transpose(0, 4, 3, 1, 2))
    outs = {"yT": (P, KT, TOK), "ret_p": (L * RH, RD, RD), "c_p": (L * MH, MQK, MV), "n_p": (L, MQK, MH),
            "m_p": (L, MH, 1), "pool_p": (L, P, PG, PBUF), "ret_s": (L * RH, RD, BATCH_S, RD),
            "c_s": (L * MH, MQK, BATCH_S, MV), "n_s": (L, MQK, MH, BATCH_S), "m_s": (L, MH, BATCH_S),
            "pool_s": (L, P, PG, BATCH_S, 16)}

    nc = bacc.Bacc("TRN2", target_bir_lowering=False, num_devices=1)
    aps = {n: nc.dram_tensor(n, v.shape, F32, kind="ExternalInput").ap() for n, v in arrays.items()}
    aps |= {n: nc.dram_tensor(n, s, F32, kind="ExternalOutput").ap() for n, s in outs.items()}
    build(nc, aps, gamma, gchunk)
    r = run_bass_kernel_spmd(nc, [arrays], core_ids=[0]).results[0]

    y = r["yT"].transpose(2, 1, 0).reshape(TOK, D_MODEL)
    return (c(y[None, 0:SEQ]), c(y[SEQ:, None]),
            c(r["ret_p"].reshape(L, 1, RH, RD, RD)), c(r["c_p"].reshape(L, 1, MH, MQK, MV)),
            c(r["n_p"].transpose(0, 2, 1)[:, None]), c(r["m_p"].reshape(L, 1, MH)),
            c(r["pool_p"].transpose(0, 3, 2, 1).reshape(L, 1, PBUF, PG * P)),
            c(r["ret_s"].reshape(L, RH, RD, BATCH_S, RD).transpose(0, 3, 1, 2, 4)),
            c(r["c_s"].reshape(L, MH, MQK, BATCH_S, MV).transpose(0, 3, 1, 2, 4)),
            c(r["n_s"].transpose(0, 3, 2, 1)), c(r["m_s"].transpose(0, 2, 1)),
            c(r["pool_s"][:, :, :, :, 1:16].transpose(0, 3, 4, 2, 1).reshape(L, BATCH_S, PBUF, PG * P)))
```

```python
from contextlib import ExitStack

import numpy as np
import concourse.bass as bass
from concourse import mybir

F32 = mybir.dt.float32
F32R = mybir.dt.float32r
ALU = mybir.AluOpType
ACT = mybir.ActivationFunctionType
AX = mybir.AxisListType

P = 128
D_MODEL, BATCH_S, SEQ, DEPTH, PAST = 2048, 8, 256, 2, 2048
TOK = SEQ + BATCH_S
CH = 128
KT = D_MODEL // P
RH, RD = 6, 128
MH, MQK, MV = 4, 96, 192
PG, PBUF = 4, 15
D_FF = ((8 * D_MODEL + 3 * 256 - 1) // (3 * 256)) * 256
FT = D_FF // P
NBLK = 2
BT = FT // NBLK
HT = BT // 2
EPS = 1e-6

T_MQ, T_MK, T_MV, T_R, T_PU, T_MO, T_RG = 0, 4, 8, 14, 32, 36, 42
NPROJ = 48


def T_RV(h):
    return T_R + 3 * h


def T_RK(h):
    return T_R + 3 * h + 1


def T_RQ(h):
    return T_R + 3 * h + 2


SCHEDULE = {1: [("gates", 0)], 2: [("log_f", 0)], 3: [("maxima", 0)], 4: [("rows", 0)], 5: [("gate_columns", 0)],
            8: [("scale_keys", 0)], 12: [("ml_values", 0)], 14: [("ml_values", 1)],
            6: [("rope_tables", 0)], 27: [("ml_sum", 0)], 28: [("ml_norm", 0)], 42: [("ml_split", 5), ("ret_sum", 0)],
            43: [("ret_norm", 0), ("ret_silu", 0), ("ret_silu", 1)],
            44: [("ret_norm", 1), ("ret_silu", 2), ("ret_product", 0), ("ret_product", 1), ("ret_split", 0),
                 ("ret_split", 1)],
            45: [("ret_silu", 3), ("ret_product", 2), ("ret_product", 3), ("pool_mix", 0)],
            46: [("ret_silu", 4), ("ret_product", 4), ("pool_split", 0), ("ret_split", 2), ("ret_split", 3),
                 ("ret_split", 4)],
            47: [("ret_split", 5)]}
EARLY = {47: [("ret_silu", 5), ("ret_last_product", 5)]}
for _h in range(MH):
    for _k, _step in enumerate(("ml_scores", "ml_states", "ml_outputs")):
        SCHEDULE[15 + 3 * _h + _k] = [(_step, _h)]
for _h in range(RH):
    SCHEDULE.setdefault(29 + 2 * _h, []).append(("ret_scores", _h))
    SCHEDULE.setdefault(30 + 2 * _h, []).append(("ret_states", _h))
    SCHEDULE.setdefault(31 + 2 * _h, []).append(("ret_outputs", _h))
for _g in range(PG):
    SCHEDULE[36 + _g].append(("pool_windows", _g))
for _j in range(6):
    SCHEDULE[36 + _j].append(("ml_sigmoid", _j))
    if _j < 5:
        SCHEDULE.setdefault(37 + _j, []).append(("ml_split", _j))
MIX_LO = [T_RQ(h) for h in range(RH)] + [T_MV + j for j in range(6)] + [T_PU + g for g in range(PG)]
MIX_HI = [T_RG + h for h in range(RH)] + [T_MO + j for j in range(6)] + [g for g in range(PG)]

CHUNK = KT * P
HALF = HT * P
C_IN, C_OUT = 0, NPROJ
C_GU = [64, 140]
C_DN = [108, 184]
N_CHUNKS = 216
O_IN, O_OUT = 0, 48
O_GU = [64, 124]
O_DN = [108, 168]
N_TILES = 184
RAW = 4
HI = 2
LEAD = 3
BANKS = 4
assert C_OUT + KT == C_GU[0] and C_GU[0] + 2 * BT == C_DN[0] and C_DN[0] + 2 * KT == C_GU[1]
assert C_DN[1] + 2 * KT == N_CHUNKS and N_CHUNKS % RAW == 0 and N_TILES % BANKS == 0

G_PREMIX, G_POSTMIX, G_PREFFN, G_POSTFFN, G_RET, G_ML, G_PS, N_GAINS = 0, 16, 32, 48, 64, 70, 76, 80


def tables():
    f = np.float32
    half = RD // 2
    inv = f(10000.0) ** (-np.arange(half, dtype=f) / f(half))
    pos = np.concatenate([np.arange(SEQ, dtype=f), np.full(BATCH_S, PAST, f)])
    ang = (pos[None, :] * inv[:, None]).astype(f)
    cos, sin = np.cos(ang.astype(np.float64)), np.sin(ang.astype(np.float64))
    c2, s2 = np.concatenate([cos, cos]), np.concatenate([sin, -sin])
    sc = RD ** -0.5
    rope = np.stack([c2, s2, c2 * sc, s2 * sc], 1).astype(f)
    lg = np.log1p(-np.exp2(-5.0 - np.arange(RH)))
    i = np.arange(CH)
    diff = i[None, :] - i[:, None]
    dec = np.where(diff[:, None, :] >= 0, np.exp(lg[None, :, None] * np.maximum(diff, 0)[:, None, :]), 0.0)
    decq = np.broadcast_to(np.exp(lg[:, None] * (i + 1.0))[None], (P, RH, CH))
    deck = np.exp(lg[None, :] * (CH - 1.0 - i)[:, None])
    ident = np.eye(P)
    ones = np.ones((P, P))
    mask = np.where(diff >= 0, 0.0, -1e30)
    sel = np.zeros((P, MH, P))
    for h in range(MH):
        sel[h, h] = 1.0
    m8 = np.zeros((P, BATCH_S))
    m8[:BATCH_S] = np.eye(BATCH_S)
    invc = np.zeros((P, PG, 16))
    for g in range(PG):
        invc[:, g] = 1.0 / np.minimum(np.arange(16) + 1.0, 2.0 ** (g + 1))
    parts = [rope, dec, decq, deck, ident, ones, mask, sel, m8, invc]
    flat = np.concatenate([np.ascontiguousarray(a.astype(f)).reshape(P, -1) for a in parts], 1)
    gamma = [float(np.exp(v)) for v in lg]
    gchunk = [float(np.exp(v * CH)) for v in lg]
    return np.ascontiguousarray(flat), gamma, gchunk


TABLE_SIZES = [4 * TOK, RH * CH, RH * CH, RH, P, P, P, MH * P, BATCH_S, PG * 16]


class Count:

    def __init__(self, sem, unit=1, head=0):
        self.sem, self.unit, self.head = sem, unit, head
        self.up = (sem, unit)

    def __call__(self, n):
        return self.sem, (n + self.head) * self.unit


class Chain:

    def __init__(self, eng, count, layer, per_layer):
        self.eng, self.count, self.base, self.k, self.per_layer = eng, count, layer * per_layer, 0, per_layer

    def __call__(self, ins):
        ins.then_inc(*self.count.up)
        self.k += 1
        self.eng.wait_ge(*self.count(self.base + self.k))
        return ins

    def close(self):
        assert self.k == self.per_layer, (self.k, self.per_layer)


def build(nc, a, gamma, gchunk):
    with ExitStack() as ctx:
        used = [0]
        arena = ctx.enter_context(nc.sbuf_tensor("arena", [P, 212800 // 4], F32))
        base0 = nc.sbuf_base() if callable(nc.sbuf_base) else nc.sbuf_base
        start = base0 - 212800

        def place(name, shape, dt, at=None):
            n = 4
            for s in shape[1:]:
                n *= s
            if at is None:
                at = used[0]
                used[0] += (n + 31) // 32 * 32
                assert used[0] <= 212800, (name, used[0])
            t = nc.alloc_sbuf_tensor_at(name, shape, dt, offset=start + at)
            return t, at

        def psum(name):
            return ctx.enter_context(nc.psum_tensor(name, [P, 512], F32))

        def sem(name):
            return ctx.enter_context(nc.semaphore(name))

        x, _ = place("x", [P, KT, TOK], F32)
        ahi, _ = place("ahi", [P, KT, TOK], F32R)
        alo, _ = place("alo", [P, KT, TOK], F32R)
        raw, at_raw = place("raw", [P, RAW, CHUNK], F32)
        wlo, _ = place("wlo", [P, RAW, CHUNK], F32R, at_raw)
        whi, _ = place("whi", [P, HI, CHUNK], F32R)
        proj, at_proj = place("proj", [P, NPROJ, TOK], F32)
        mixed, _ = place("mixed", [P, NPROJ, TOK], F32R, at_proj)
        hhi, _ = place("hhi", [P, BT, TOK], F32R, at_proj)
        hlo, _ = place("hlo", [P, BT, TOK], F32R, at_proj + 4 * BT * TOK)
        table, _ = place("table", [P, sum(TABLE_SIZES)], F32)
        gains, _ = place("gains", [P, DEPTH, N_GAINS], F32)
        wpool, _ = place("wpool", [P, PG, P], F32)
        gbias, _ = place("gbias", [P, DEPTH, 2], F32)
        sq, _ = place("sq", [P, 4, TOK], F32)
        ssq, _ = place("ssq", [P, TOK], F32)
        rms, _ = place("rms", [P, TOK], F32)
        rstd, _ = place("rstd", [P, TOK], F32)
        epsc, _ = place("epsc", [P, 1], F32)
        unread, _ = place("unread", [P, 1], F32)
        zero, _ = place("zero", [P, TOK], F32)
        WORK = (212800 - used[0]) // 4 - 8
        work, at_work = place("work", [P, WORK], F32)
        acc = work[:, 0:KT * TOK].rearrange("p (k t) -> p k t", k=KT)

        def carve(region, at, *shapes):
            out = []
            for shape in shapes:
                n = 1
                for d in shape:
                    n *= d
                v = region[:, at:at + n]
                at += n
                if len(shape) == 2:
                    v = v.rearrange("p (a b) -> p a b", a=shape[0])
                if len(shape) == 3:
                    v = v.rearrange("p (a b c) -> p a b c", a=shape[0], b=shape[1])
                out.append(v)
            assert at <= region.shape[1], (at, region.shape)
            return out + [at]

        ga, sg, ua, hs, at_spare = carve(work, KT * TOK, (2, TOK), (2, TOK), (2, TOK), (2, TOK))
        whi_spare, _ = place("whi_spare", [P, CHUNK], F32R, at_work + 4 * at_spare)
        assert at_spare + CHUNK <= WORK
        S, rot, at_m = carve(work, 0, (2, BATCH_S, CH), (2, TOK))
        NR2 = CH + 3 * BATCH_S
        (mvtok, mvs, lft, bcum, gpre, mrun, mst, rows1, rows2, wT, en, ab, msT, kw, aq, gcol, C1, C2, n1, n2, nrep,
         nsn, qn, kws, kst, m0s, mfin, mss, w8, _) = carve(
            work, at_m, (2, MV * MH), (MV * MH,), (TOK,), (TOK,), (TOK,), (TOK,), (TOK,), (2 * SEQ,), (NR2,), (2, CH),
            (TOK,), (NR2,), (2, CH), (2, MQK), (CH,), (2, MH), (MV,), (MV,), (2,), (MH,), (P,), (MH, BATCH_S),
            (BATCH_S,), (BATCH_S,), (MQK,), (BATCH_S,), (2,), (BATCH_S,), (BATCH_S,))
        PW = SEQ + 16
        vtok, ktok, vks, vdiag, S1, S2, sT, qdec, at_r = carve(
            work, at_m, (2, CH), (2, CH), (2, CH), (BATCH_S, CH), (CH,), (CH,), (2, CH), (CH,))
        pa, pb, cut16, pwin, wsum, _ = carve(work, at_r, (PW,), (PW,), (16,), (PG, BATCH_S * 16), (PG, BATCH_S))
        pwin = pwin.rearrange("p g (b i) -> p g b i", b=BATCH_S)
        flat_sq = sq[:].rearrange("p a t -> p (a t)")
        gates, lfa, lfb, _ = carve(flat_sq, 0, (2, TOK), (TOK,), (TOK,))
        late = proj[:, T_MO:NPROJ, :].rearrange("p a t -> p (a t)")
        Cs, cdiag, _ = carve(late, 0, (BATCH_S, MV), (BATCH_S, MV))
        ropes = proj[:, T_PU:T_PU + 4, :]

        o = [0]
        for n in TABLE_SIZES:
            o.append(o[-1] + n)
        view = [table[:, o[i]:o[i + 1]] for i in range(len(TABLE_SIZES))]
        rope = view[0].rearrange("p (a t) -> p a t", a=4)
        dec = view[1].rearrange("p (h t) -> p h t", h=RH)
        decq = view[2].rearrange("p (h t) -> p h t", h=RH)
        deck, ident, ones, mask = view[3:7]
        sel = view[7].rearrange("p (h m) -> p h m", h=MH)
        m8 = view[8]
        invc = view[9].rearrange("p (g i) -> p g i", g=PG)

        bank = [psum(f"bank{i}") for i in range(8)]

        def cnt(name, unit=1, head=0):
            c = Count(sem(name), unit, head)
            if head:
                ahead.append(c)
            return c

        ahead = []
        raw_landed = [cnt(f"raw_landed{i}", 16) for i in range(RAW)]
        x_landed = [cnt(f"x_landed{i}", 16) for i in range(4)]
        const_landed = cnt("const_landed", 16)
        hi_made = cnt("hi_made")
        chunk_split = cnt("chunk_split")
        chunk_used = cnt("chunk_used", head=RAW)
        tile_evac = cnt("tile_evac", head=BANKS)
        operand_hi, operand_lo = cnt("operand_hi"), cnt("operand_lo")
        mixed_ready = cnt("mixed_ready")
        scaled = cnt("scaled")
        x_updated = cnt("x_updated", head=KT)
        sqx_made, sqx_used = cnt("sqx_made"), cnt("sqx_used", head=4)
        sq_made, sq_added = cnt("sq_made"), cnt("sq_added", head=4)
        ssq_summed, rms_made, rstd_made = cnt("ssq_summed", head=1), cnt("rms_made", head=1), cnt("rstd_made", head=1)
        silu_made = cnt("silu_made", head=2)
        hidden_made = cnt("hidden_made", head=2)
        hidden_hi = cnt("hidden_hi", head=2)
        hidden_ready = cnt("hidden_ready")
        dve_done, act_done, pool_done = cnt("dve_done"), cnt("act_done"), cnt("pool_done")
        ropes_made = cnt("ropes_made")
        rotated = cnt("rotated", head=1)
        (ret_turned, ret_scored, ret_vk, ret_vks, ret_weighted, ret_diag, ret_grown, ret_outer, ret_s1, ret_out,
         ret_last_gated, ret_summed, ret_rms, ret_inv, ret_spread, ret_normed, ret_silu, ret_gated, ret_hi) = (
            cnt(n) for n in ("ret_turned ret_scored ret_vk ret_vks ret_weighted ret_diag ret_grown ret_outer ret_s1 "
                             "ret_out ret_last_gated ret_summed ret_rms ret_inv ret_spread ret_normed ret_silu ret_gated "
                             "ret_hi").split())
        ret_s2, ret_snew, ret_kept = cnt("ret_s2", head=1), cnt("ret_snew", head=1), cnt("ret_kept", head=1)
        S_landed, S_stored = [cnt(f"S_landed{i}", 16) for i in range(2)], [cnt(f"S_stored{i}", 16) for i in range(2)]
        S2_stored = cnt("S2_stored", 16)
        (ml_abs, ml_log, ml_rows, ml_a1, ml_row2, ml_gturn, ml_gcol, ml_vturned, ml_vtok, ml_scored, ml_weights, ml_w8,
         ml_keys, ml_grown, ml_c1, ml_outer, ml_diag, ml_decayed, ml_num, ml_sq, ml_summed, ml_rms, ml_inv, ml_spread,
         ml_normed, ml_sig, ml_gated, ml_hi, ml_scaled) = (
            cnt(n) for n in ("ml_abs ml_log ml_rows ml_a1 ml_row2 ml_gturn ml_gcol ml_vturned ml_vtok ml_scored "
                             "ml_weights ml_w8 ml_keys ml_grown ml_c1 ml_outer ml_diag ml_decayed ml_num ml_sq "
                             "ml_summed ml_rms ml_inv ml_spread ml_normed ml_sig ml_gated ml_hi ml_scaled").split())
        ml_c2, ml_cs, ml_h = cnt("ml_c2", head=1), cnt("ml_cs", head=1), cnt("ml_h", head=1)
        C_landed, C_stored, C2_stored = cnt("C_landed", 16), cnt("C_stored", 16), cnt("C2_stored", 16)
        n_landed, m_landed, wpool_landed = cnt("n_landed", 16), cnt("m_landed", 16), cnt("wpool_landed", 16)
        m_stored, n_stored = cnt("m_stored", 16), cnt("n_stored", 16)
        pl_landed, pl_copied, pl_win, pl_y, pl_hi = (cnt("pl_landed", 16), cnt("pl_copied"), cnt("pl_win"),
                                                     cnt("pl_y", head=1), cnt("pl_hi"))
        pl_z, plp_stored, pls_stored = cnt("pl_z", head=1), cnt("plp_stored", 16), cnt("pls_stored", 16)
        y_stored = cnt("y_stored", 16)

        passed = {}

        def apart(eng):
            eng.sem_inc(passed[eng.engine], 1)

        for engine in (nc.tensor, nc.vector, nc.gpsimd):
            passed[engine.engine] = sem(f"passed_{len(passed)}")
        block = ctx.enter_context(nc.Block())

        @block.sync
        def _(sp):
            for i in range(4):
                sp.dma_start(x[:, 4 * i:4 * i + 4, :], a["xT"][:, 4 * i:4 * i + 4, :]).then_inc(*x_landed[i].up)
            with sp.Fori(0, DEPTH) as l:

                def load(n, slot, src, words):
                    sp.wait_ge(*chunk_used(n - RAW + 1))
                    sp.dma_start(raw[:, slot, 0:words], src).then_inc(*raw_landed[slot].up)

                with sp.Fori(0, NPROJ // RAW) as i:
                    for j in range(RAW):
                        load(l * N_CHUNKS + C_IN + i * RAW + j, j, a["w_in"][l * NPROJ + i * RAW + j], CHUNK)
                with sp.Fori(0, KT // RAW) as i:
                    for j in range(RAW):
                        load(l * N_CHUNKS + C_OUT + i * RAW + j, j, a["w_out"][l * KT + i * RAW + j], CHUNK)
                for b in range(NBLK):
                    with sp.Fori(0, 2 * BT // RAW) as i:
                        for j in range(RAW):
                            load(l * N_CHUNKS + C_GU[b] + i * RAW + j, j,
                                 a["w_gu"][l * 2 * FT + b * 2 * BT + i * RAW + j], CHUNK)
                    with sp.Fori(0, 2 * KT // RAW) as i:
                        for j in range(RAW):
                            load(l * N_CHUNKS + C_DN[b] + i * RAW + j, j,
                                 a["w_dn"][(l * NBLK + b) * 2 * KT + i * RAW + j], HALF)
            for i in range(4):
                sp.wait_ge(*x_updated(DEPTH * 2 * KT - KT + 4 * i + 4))
                sp.dma_start(a["yT"][:, 4 * i:4 * i + 4, :], x[:, 4 * i:4 * i + 4, :]).then_inc(*y_stored.up)
            sp.wait_ge(*y_stored(4))

        @block.tensor
        def _(pe):
            pe.wait_ge(*const_landed(3))
            with pe.Fori(0, DEPTH) as l:

                def acc_sum(e):
                    pe.wait_ge(*sq_added(l * 32 + (e // 2) * KT + KT))
                    pe.wait_ge(*rms_made(l * 4 + e))
                    pe.matmul(bank[4][:, 0:TOK], ones, ssq[:], start=True, stop=True).then_inc(*ssq_summed.up)

                def chunk(n, slot, out, operand, ks, start, stop, fresh=None, spare=False, last_ready=None):
                    pe.wait_ge(*chunk_split(n + 1))
                    if fresh:
                        pe.wait_ge(*rms_made(l * 4 + fresh[0]))
                    high = whi_spare if spare else whi[:, slot % HI]
                    for k, tile in enumerate(ks):
                        w = bass.ds((tile - min(ks)) * P, P)
                        hi, lo = operand(tile)
                        first, last = start and k == 0, stop and k == len(ks) - 1
                        if last and last_ready:
                            pe.wait_ge(*last_ready)
                        if fresh:
                            kk = l * 2 * KT + fresh[1] * KT + k
                            pe.wait_ge(*sqx_made(kk + 1))
                            mm = pe.matmul(bank[4][:, 0:TOK], ones, sq[:, k % 4, :], start=k == 0, stop=k == KT - 1)
                            mm.then_inc(*sqx_used.up)
                            pe.wait_ge(*operand_lo(kk + 1))
                        pe.matmul(out, high[:, w], hi, start=first, stop=False)
                        pe.matmul(out, high[:, w], lo, start=False, stop=False)
                        mm = pe.matmul(out, wlo[:, slot, w], hi, start=False, stop=last)
                    mm.then_inc(*chunk_used.up)

                def of_x(k):
                    return ahi[:, k, :], alo[:, k, :]

                def of_mixers(k):
                    return mixed[:, MIX_HI[k], :], mixed[:, MIX_LO[k], :]

                def of_hidden(k):
                    return hhi[:, k, :], hlo[:, k, :]

                def whole_tile(c, o, j, operand, fresh=None, spare=False):
                    pe.wait_ge(*tile_evac(o - BANKS + 1))
                    chunk(c, j, bank[j][:, 0:TOK], operand, range(KT), True, True, fresh, spare)

                def whole(first, bodies, c0, o0, operand):
                    apart(pe)
                    with pe.Fori(first, bodies) as i:
                        for j in range(RAW):
                            whole_tile(l * N_CHUNKS + c0 + i * RAW + j, l * N_TILES + o0 + i * RAW + j, j, operand)

                def turn(out, in_, n=P):
                    return pe.matmul(out, in_, ident[0:n, 0:n], is_transpose=True, start=True, stop=True)

                def gate_columns(_):
                    pe.wait_ge(*ml_rows(l + 1))
                    apart(pe)
                    for c in range(2):
                        mm = turn(bank[5][:, c * MH:(c + 1) * MH], gpre[0:MH, c * CH:(c + 1) * CH], MH)
                    mm.then_inc(*ml_gturn.up)

                def ml_values(part):
                    if part == 0:
                        pe.wait_ge(*ml_gcol(l + 1))
                    else:
                        pe.wait_ge(*ml_vtok(2 * l + 1))
                    pe.wait_ge(*tile_evac(l * N_TILES + T_MV + 3 * part + 3))
                    for i in range(3):
                        t = T_MV + 3 * part + i
                        for c in range(2):
                            turn(bank[4 + i // 2][:, (i % 2 * 2 + c) * P:(i % 2 * 2 + c + 1) * P], proj[:, t, c * CH:(c + 1) * CH])
                        mm = turn(bank[6][0:BATCH_S, i * P:(i + 1) * P], proj[:, t, SEQ:TOK])
                    mm.then_inc(*ml_vturned.up)

                def ml_scores(h):
                    q = l * MH + h
                    qt, kt_ = proj[0:MQK, T_MQ + h, :], proj[0:MQK, T_MK + h, :]
                    if h == 0:
                        pe.wait_ge(*ml_vtok(2 * l + 2))
                        pe.wait_ge(*ml_row2(l + 1))
                        pe.wait_ge(*ml_scaled(l + 1))
                    pe.wait_ge(*ml_h(q))
                    pe.wait_ge(*ml_c2(q))
                    pe.matmul(bank[4][:, 0:2 * SEQ], sel[0:MH, h, :], rows1[0:MH, :], start=True, stop=False,
                              skip_group_check=True)
                    for c in range(2):
                        pe.matmul(bank[4][:, c * CH:(c + 1) * CH], ident, mask, start=False, stop=(c == 1),
                                  skip_group_check=True)
                    pe.matmul(bank[5][:, 0:NR2], sel[0:MH, h, :], rows2[0:MH, :], start=True, stop=True)
                    for c in range(2):
                        turn(bank[6][:, c * MQK:(c + 1) * MQK], kt_[:, c * CH:(c + 1) * CH], MQK)
                    turn(bank[6][0:BATCH_S, 2 * MQK:3 * MQK], kt_[:, SEQ:TOK], MQK)
                    for c in range(2):
                        t = slice(c * CH, (c + 1) * CH)
                        mm = pe.matmul(bank[7][:, t], kt_[:, t], qt[:, t], start=True, stop=True)
                    mm.then_inc(*ml_scored.up)

                def ml_states(h):
                    q = l * MH + h
                    pe.wait_ge(*ml_keys(q + 1))
                    for c in range(2):
                        pe.matmul(bank[6][0:MQK, c * MV:(c + 1) * MV], kw[:, c, :], mvtok[:, c, h * MV:(h + 1) * MV],
                                  start=True, stop=True)
                        mm = pe.matmul(bank[6][0:MQK, 400 + c:401 + c], kw[:, c, :], ones[:, 0:1], start=True, stop=True)
                    mm.then_inc(*ml_grown.up)
                    pe.wait_ge(*ml_diag(q + 1))
                    pe.wait_ge(*ml_weights(q + 1))
                    flat = cdiag[0:BATCH_S].rearrange("p b v -> p (b v)")
                    for i, bk in enumerate((4, 5, 7)):
                        mm = pe.matmul(bank[bk][0:MQK, :], kst[0:BATCH_S, :], flat[:, 512 * i:512 * (i + 1)],
                                       start=True, stop=True)
                    mm.then_inc(*ml_outer.up)

                def ml_outputs(h):
                    q = l * MH + h
                    odd = h % 2
                    qt = proj[0:MQK, T_MQ + h, :]
                    pe.wait_ge(*ml_c1(q + 1))
                    pe.wait_ge(*ml_cs(q + 1))
                    big, small = ((64, MV), (0, 64)) if odd else ((0, P), (P, MV))
                    v0 = h * MV
                    for bk, (f0, f1), po in ((4, big, 0), (5, small, 64 * odd)):
                        rows = slice(po, po + f1 - f0)
                        pe.matmul(bank[bk][rows, 0:CH], mvtok[:, 0, v0 + f0:v0 + f1], msT[:, 0, :], start=True, stop=True)
                        pe.matmul(bank[bk][rows, CH:SEQ], mvtok[:, 1, v0 + f0:v0 + f1], msT[:, 1, :], start=True, stop=False)
                        pe.matmul(bank[bk][rows, CH:SEQ], C1[0:MQK, f0:f1], aq[0:MQK, :], start=False, stop=True)
                        for b in range(BATCH_S):
                            pe.matmul(bank[bk][rows, SEQ + b:SEQ + b + 1], Cs[0:MQK, b, f0:f1], qt[:, SEQ + b:SEQ + b + 1],
                                      start=True, stop=True)
                    pe.matmul(bank[7][:, 0:CH], ones, msT[:, 0, :], start=True, stop=True)
                    pe.matmul(bank[7][:, CH:SEQ], ones, msT[:, 1, :], start=True, stop=False)
                    pe.matmul(bank[7][:, CH:SEQ], nrep[0:MQK, :], aq[0:MQK, :], start=False, stop=True)
                    pe.matmul(bank[7][:, SEQ:TOK], ones[0:MQK, :], qn[0:MQK, :], start=True, stop=True)\
                        .then_inc(*ml_num.up)

                def ml_sum(_):
                    pe.wait_ge(*ml_sq(l + 1))
                    for h in range(MH):
                        odd, t0 = h % 2, 3 * (h // 2)
                        out = bank[4][32 * h:32 * h + 32, 0:TOK]
                        if not odd:
                            pe.matmul(out, ones[:, 0:32], proj[:, t0, :], start=True, stop=False)
                            mm = pe.matmul(out, ones[0:64, 0:32], proj[0:64, t0 + 1, :], start=False, stop=True)
                        else:
                            pe.matmul(out, ones[64:128, 0:32], proj[64:128, t0 + 1, :], start=True, stop=False)
                            mm = pe.matmul(out, ones[:, 0:32], proj[:, t0 + 2, :], start=False, stop=True)
                    mm.then_inc(*ml_summed.up)

                def ml_norm(_):
                    pe.wait_ge(*ml_inv(l + 1))
                    for h in range(MH):
                        mm = pe.matmul(bank[4 + h][:, 0:TOK], ones[32 * h:32 * h + 1, :], proj[32 * h:32 * h + 1, 7, :],
                                       start=True, stop=True)
                    mm.then_inc(*ml_spread.up)

                def ret_scores(h):
                    r = l * RH + h
                    if h == 0:
                        pe.wait_ge(*ml_normed(l + 1))
                    pe.wait_ge(*rotated(2 * r + 2))
                    pe.wait_ge(*ret_snew(r))
                    v, k, q = (proj[:, T(h), :] for T in (T_RV, T_RK, T_RQ))
                    for c in range(2):
                        turn(bank[4][:, c * CH:(c + 1) * CH], v[:, c * CH:(c + 1) * CH])
                        turn(bank[4][:, (2 + c) * CH:(3 + c) * CH], k[:, c * CH:(c + 1) * CH])
                    turn(bank[5][0:BATCH_S, 0:P], v[:, SEQ:TOK])
                    turn(bank[5][0:BATCH_S, P:2 * P], k[:, SEQ:TOK]).then_inc(*ret_turned.up)
                    for c in range(2):
                        t = slice(c * CH, (c + 1) * CH)
                        mm = pe.matmul(bank[6][:, t], k[:, t], q[:, t], start=True, stop=True)
                    mm.then_inc(*ret_scored.up)

                def ret_states(h):
                    r = l * RH + h
                    pe.wait_ge(*ret_vk(r + 1))
                    pe.wait_ge(*ret_kept(r))
                    for c in range(2):
                        mm = pe.matmul(bank[7][:, c * CH:(c + 1) * CH], ktok[:, c, :], vtok[:, c, :], start=True, stop=True)
                    mm.then_inc(*ret_grown.up)
                    pe.wait_ge(*ret_diag(r + 1))
                    for i in range(2):
                        mm = pe.matmul(bank[4 + i][:, 0:512], vks[0:BATCH_S, 1, :],
                                       vdiag[0:BATCH_S, 4 * i:4 * i + 4, :].rearrange("p b v -> p (b v)"),
                                       start=True, stop=True)
                    mm.then_inc(*ret_outer.up)

                def ret_outputs(h):
                    r = l * RH + h
                    q = proj[:, T_RQ(h), :]
                    pe.wait_ge(*ret_weighted(r + 1))
                    pe.wait_ge(*ret_s2(r + 1))
                    pe.matmul(bank[7][:, 0:CH], vtok[:, 0, :], sT[:, 0, :], start=True, stop=True)
                    pe.matmul(bank[7][:, CH:SEQ], vtok[:, 1, :], sT[:, 1, :], start=True, stop=False)
                    pe.matmul(bank[7][:, CH:SEQ], S1, qdec, start=False, stop=True)
                    pe.wait_ge(*ret_snew(r + 1))
                    for b in range(BATCH_S):
                        mm = pe.matmul(bank[7][:, SEQ + b:SEQ + b + 1], S[:, h % 2, b, :], q[:, SEQ + b:SEQ + b + 1],
                                       start=True, stop=True)
                    mm.then_inc(*ret_out.up)

                def ret_sum(_):
                    pe.wait_ge(*ret_kept(l * RH + RH))
                    for h in range(RH):
                        mm = pe.matmul(bank[4 + h // 4][32 * (h % 4):32 * (h % 4) + 32, 0:TOK], ones[:, 0:32],
                                       proj[:, T_RK(h), :], start=True, stop=True)
                    mm.then_inc(*ret_summed.up)

                def ret_norm(part):
                    if part == 0:
                        pe.wait_ge(*ret_inv(l + 1))
                    else:
                        pe.wait_ge(*ret_normed(2 * l + 1))
                    for h in range(4) if part == 0 else (4, 5):
                        row = 32 * (h % 4)
                        mm = pe.matmul(bank[4 + h % 4][:, 0:TOK], ones[row:row + 1, :], proj[row:row + 1, 2 + part, :],
                                       start=True, stop=True)
                    mm.then_inc(*ret_spread.up)

                def pool_mix(_):
                    pe.wait_ge(*wpool_landed(l + 1))
                    pe.wait_ge(*ret_normed(2 * l + 2))
                    pe.wait_ge(*pl_z(l * PG + PG))
                    for g in range(PG):
                        mm = pe.matmul(bank[4 + g][:, 0:TOK], wpool[:, g, :], proj[:, T_PU + g, :], start=True, stop=True)
                    mm.then_inc(*pl_y.up)

                steps = {"gate_columns": gate_columns, "ml_values": ml_values, "ml_scores": ml_scores,
                         "ml_states": ml_states, "ml_outputs": ml_outputs, "ml_sum": ml_sum, "ml_norm": ml_norm,
                         "ret_scores": ret_scores, "ret_states": ret_states, "ret_outputs": ret_outputs,
                         "ret_sum": ret_sum, "ret_norm": ret_norm, "pool_mix": pool_mix}

                for n in range(NPROJ):
                    whole_tile(l * N_CHUNKS + n, l * N_TILES + n, n % RAW, of_x, (0, 0) if n == 0 else None)
                    for name, arg in SCHEDULE.get(n, ()):
                        if name in steps:
                            steps[name](arg)

                for j in range(RAW):
                    c, o_ = l * N_CHUNKS + C_OUT + j, l * N_TILES + O_OUT + j
                    if j == 0:
                        pe.wait_ge(*tile_evac(o_ - BANKS + 1))
                        pe.wait_ge(*mixed_ready(2 * l + 1))
                        chunk(c, j, bank[j][:, 0:TOK], of_mixers, [k for k in range(KT) if k != RH - 1] + [RH - 1],
                              True, True, last_ready=mixed_ready(2 * l + 2))
                    else:
                        whole_tile(c, o_, j, of_mixers)
                whole(1, KT // RAW, C_OUT, O_OUT, of_mixers)
                acc_sum(1)
                for b in range(NBLK):
                    if b == 0:
                        for j in range(RAW):
                            whole_tile(l * N_CHUNKS + C_GU[0] + j, l * N_TILES + O_GU[0] + j, j, of_x,
                                       (2, 1) if j == 0 else None, spare=j == 1)
                    whole(1 if b == 0 else 0, 2 * BT // RAW, C_GU[b], O_GU[b], of_x)
                    with pe.Fori(0, KT // 4) as i:
                        for j in range(8):
                            u, half = j // 2, j % 2
                            if j < 2:
                                pe.wait_ge(*hidden_ready(l * FT + b * BT + (half + 1) * HT))
                            if half == 0:
                                pe.wait_ge(*tile_evac(l * N_TILES + O_DN[b] + i * 4 + u - BANKS + 1))
                            chunk(l * N_CHUNKS + C_DN[b] + i * 8 + j, j % RAW, bank[u][:, 0:TOK], of_hidden,
                                  range(half * HT, (half + 1) * HT), half == 0, half == 1)
                acc_sum(3)

        @block.scalar
        def _(act):
            act.dma_start(gains[:], a["gains"]).then_inc(*const_landed.up)
            act.dma_start(table[:], a["table"]).then_inc(*const_landed.up)
            act.dma_start(gbias[0:MH], a["gbias"]).then_inc(*const_landed.up)
            act.wait_ge(*const_landed(3))
            act.wait_ge(*dve_done(2))
            for i in range(4):
                act.wait_ge(*x_landed[i](1))
            with act.Fori(0, DEPTH) as l:

                def hi_part(n, slot, words, spare=False):
                    act.wait_ge(raw_landed[slot].sem, (n - slot) * 4 + 16)
                    if not spare:
                        act.wait_ge(*chunk_used(n - HI + 1))
                    high = whi_spare if spare else whi[:, slot % HI]
                    act.activation(high[:, 0:words], raw[:, slot, 0:words], ACT.Copy).then_inc(*hi_made.up)

                def load_sqrt_table():
                    act.activation(unread[:], epsc[:], ACT.Sqrt)

                def square_acc(m, k, slot):
                    act.wait_ge(*sq_added(l * 32 + m * KT + k - 3))
                    act.activation(sq[:, slot, :], acc[:, k, :], ACT.Square).then_inc(*sq_made.up)

                def operand(m, gain):
                    for k in range(KT):
                        kk = l * 2 * KT + m * KT + k
                        act.wait_ge(*x_updated(kk - KT + 1))
                        act.wait_ge(*sqx_used(kk - 3))
                        act.activation(sq[:, k % 4, :], x[:, k, :], ACT.Square).then_inc(*sqx_made.up)
                        act.activation(ahi[:, k, :], x[:, k, :], ACT.Copy, scale=gains[:, l, gain + k:gain + k + 1])\
                            .then_inc(*operand_hi.up)

                def make_rms(e):
                    if e % 2:
                        act.wait_ge(*ssq_summed(l * 2 + e // 2 + 1))
                    else:
                        act.wait_ge(*sqx_used(l * 2 * KT + (e // 2) * KT + KT))
                    act.wait_ge(*rstd_made(l * 4 + e))
                    act.activation(rms[:], bank[4][:, 0:TOK], ACT.Sqrt, scale=1.0 / D_MODEL, bias=epsc[:])\
                        .then_inc(*rms_made.up)

                def gates_(_):
                    act.wait_ge(*ml_abs(l + 1))
                    act.activation(lfb[0:MH, :], lfa[0:MH, :], ACT.Exp).then_inc(*act_done.up)
                    act.wait_ge(*act_done(l + 1))
                    act.activation(lfb[0:MH, :], lfb[0:MH, :], ACT.Ln, bias=ones[0:MH, 0:1]).then_inc(*ml_log.up)

                def rows(_):
                    act.wait_ge(*ml_a1(l + 1))
                    act.activation(rows2[0:MH, 0:CH], rows1[0:MH, CH:SEQ], ACT.Exp, bias=mst[0:MH, CH - 1:CH])
                    act.activation(rows2[0:MH, CH:NR2], lft[0:MH, 0:3 * BATCH_S], ACT.Exp).then_inc(*ml_row2.up)

                def gate_columns(_):
                    act.wait_ge(*ml_gturn(l + 1))
                    act.activation(gcol[:], bank[5][:, 0:2 * MH].rearrange("p (c h) -> p c h", c=2), ACT.Copy)\
                        .then_inc(*ml_gcol.up)

                def ml_values(part):
                    act.wait_ge(*ml_vturned(2 * l + part + 1))
                    t = 3 * part * P
                    act.activation(mvtok[:, :, t:t + 2 * P].rearrange("p c (t f) -> p t c f", t=2),
                                   bank[4][:, :].rearrange("p (t c f) -> p t c f", t=2, c=2), ACT.Copy)
                    act.activation(mvtok[:, :, t + 2 * P:t + 3 * P], bank[5][:, 0:2 * P].rearrange("p (c f) -> p c f", c=2),
                                   ACT.Copy)
                    act.activation(mvs[0:BATCH_S, t:t + 3 * P], bank[6][0:BATCH_S, 0:3 * P], ACT.Copy).then_inc(*ml_vtok.up)

                def ml_scores(h):
                    q = l * MH + h
                    act.wait_ge(*ml_scored(q + 1))
                    act.activation(ab[:], bank[5][:, 0:NR2], ACT.Copy).then_inc(*ml_w8.up)
                    act.activation(en[:, SEQ:TOK], bank[5][:, NR2 - BATCH_S:NR2], ACT.Copy)
                    for c in range(2):
                        act.activation(wT[:, c, :], bank[4][:, c * CH:(c + 1) * CH], ACT.Exp, bias=gcol[:, c, h:h + 1])
                    act.activation(en[:, 0:SEQ], bank[4][:, SEQ:2 * SEQ], ACT.Exp).then_inc(*ml_weights.up)

                def ml_states(h):
                    act.wait_ge(*ml_grown(l * MH + h + 1))
                    act.activation(n1[0:MQK, 0:1], bank[6][0:MQK, 400:401], ACT.Copy)
                    act.activation(C1[0:MQK, :], bank[6][0:MQK, 0:MV], ACT.Copy).then_inc(*ml_c1.up)

                def ml_sum(_):
                    act.wait_ge(*ml_h(l * MH + MH))
                    act.activation(proj[:, 0:6, :], proj[:, T_MV:T_MV + 6, :], ACT.Square).then_inc(*ml_sq.up)
                    act.wait_ge(*ml_summed(l + 1))
                    act.activation(proj[:, 6, :], bank[4][:, 0:TOK], ACT.Sqrt, scale=1.0 / MV, bias=epsc[:])\
                        .then_inc(*ml_rms.up)

                def ret_scores(h):
                    r = l * RH + h
                    act.wait_ge(*ret_turned(r + 1))
                    act.activation(vks[0:BATCH_S], bank[5][0:BATCH_S, 0:2 * P].rearrange("p (c f) -> p c f", c=2),
                                   ACT.Copy).then_inc(*ret_vks.up)
                    act.activation(vtok[:], bank[4][:, 0:SEQ].rearrange("p (c f) -> p c f", c=2), ACT.Copy)
                    act.activation(ktok[:], bank[4][:, SEQ:2 * SEQ].rearrange("p (c f) -> p c f", c=2), ACT.Copy,
                                   scale=deck[:, h:h + 1]).then_inc(*ret_vk.up)

                def ret_states(h):
                    act.wait_ge(*ret_grown(l * RH + h + 1))
                    act.activation(S1, bank[7][:, 0:CH], ACT.Copy).then_inc(*ret_s1.up)

                def ret_outputs(h):
                    act.wait_ge(*ret_out(l * RH + h + 1))
                    act.activation(proj[:, T_RQ(h), :], bank[7][:, 0:TOK], ACT.Copy)
                    act.activation(proj[:, T_RK(h), :], bank[7][:, 0:TOK], ACT.Square).then_inc(*ret_kept.up)

                def ret_sum(_):
                    act.wait_ge(*ret_summed(l + 1))
                    act.activation(proj[:, 0, :], bank[4][:, 0:TOK], ACT.Sqrt, scale=1.0 / RD, bias=epsc[:])
                    act.activation(proj[0:64, 1, :], bank[5][0:64, 0:TOK], ACT.Sqrt, scale=1.0 / RD, bias=epsc[0:64])\
                        .then_inc(*ret_rms.up)

                def ml_sigmoid(j):
                    g = proj[:, T_MO + j, :]
                    act.wait_ge(*tile_evac(l * N_TILES + T_MO + j + 1))
                    act.activation(g, g, ACT.Sigmoid).then_inc(*ml_sig.up)

                def ml_split(j):
                    act.wait_ge(*ml_gated(l * 6 + j + 1))
                    act.activation(mixed[:, T_MO + j, :], proj[:, T_MV + j, :], ACT.Copy).then_inc(*ml_hi.up)

                def ret_silu_(h):
                    g = proj[:, T_RG + h, :]
                    act.wait_ge(*tile_evac(l * N_TILES + T_RG + h + 1))
                    act.activation(g, g, ACT.Silu).then_inc(*ret_silu.up)

                def ret_split(h):
                    if h < RH - 1:
                        act.wait_ge(*ret_gated(l * (RH - 1) + h + 1))
                    else:
                        act.wait_ge(*ret_last_gated(l + 1))
                    act.activation(mixed[:, T_RG + h, :], proj[:, T_RQ(h), :], ACT.Copy).then_inc(*ret_hi.up)

                def pool_windows(g):
                    u = proj[:, T_PU + g, :]
                    act.wait_ge(*tile_evac(l * N_TILES + T_PU + g + 1))
                    act.wait_ge(*pl_landed(l + 1))
                    act.wait_ge(*pl_z(l * PG + g))
                    act.activation(pwin[:, g, :, 15], u[:, SEQ:TOK], ACT.Copy)
                    act.activation(pa[:, 16:PW], u[:, 0:SEQ], ACT.Copy).then_inc(*pl_copied.up)

                def pool_mix(_):
                    act.wait_ge(*pl_y(l + 1))
                    for g in range(PG):
                        gain = gains[:, l, G_PS + g:G_PS + g + 1]
                        act.activation(proj[:, T_PU + g, :], bank[4 + g][:, 0:TOK], ACT.Copy, scale=gain)
                        last = act.activation(mixed[:, g, :], bank[4 + g][:, 0:TOK], ACT.Copy, scale=gain)
                    last.then_inc(*pl_hi.up)

                steps = {"gates": gates_, "rows": rows, "gate_columns": gate_columns, "ml_values": ml_values,
                         "ml_scores": ml_scores, "ml_states": ml_states, "ml_sum": ml_sum, "ret_scores": ret_scores,
                         "ret_states": ret_states, "ret_outputs": ret_outputs, "ret_sum": ret_sum, "ml_sigmoid": ml_sigmoid,
                         "ml_split": ml_split, "ret_silu": ret_silu_, "ret_split": ret_split,
                         "pool_windows": pool_windows, "pool_mix": pool_mix}

                c0 = l * N_CHUNKS
                hi_part(c0, 0, CHUNK)
                hi_part(c0 + 1, 1, CHUNK)
                operand(0, G_PREMIX)
                make_rms(0)
                for n in range(NPROJ):
                    for name, arg in EARLY.get(n, ()):
                        if name in steps:
                            steps[name](arg)
                    hi_part(c0 + n + HI, (n + HI) % RAW, CHUNK)
                    for name, arg in SCHEDULE.get(n, ()):
                        if name in steps:
                            steps[name](arg)

                def out_tiles(i, last):
                    for j in range(RAW):
                        act.wait_ge(*tile_evac(l * N_TILES + O_OUT + i * RAW + j + 1))
                        square_acc(0, i * RAW + j, j)
                        if not last or j < HI:
                            hi_part(c0 + C_OUT + i * RAW + j + HI, (j + HI) % RAW, CHUNK)
                        elif j == HI:
                            hi_part(c0 + C_GU[0], 0, CHUNK)
                            hi_part(c0 + C_GU[0] + 1, 1, CHUNK, spare=True)

                load_sqrt_table()
                with act.Fori(0, KT // RAW - 1) as i:
                    out_tiles(i, False)
                out_tiles(KT // RAW - 1, True)
                make_rms(1)
                operand(1, G_PREFFN)
                make_rms(2)

                for b in range(NBLK):

                    def gate_up(i, words_last):
                        for j in range(RAW):
                            u = j // 2
                            words = words_last if j >= RAW - HI else CHUNK
                            hi_part(c0 + C_GU[b] + i * RAW + j + HI, (j + HI) % RAW, words)
                            f = l * FT + b * BT + i * 2 + u
                            if j % 2 == 0:
                                act.wait_ge(*tile_evac(l * N_TILES + O_GU[b] + i * RAW + j + 1))
                                act.wait_ge(*hidden_made(f - 1))
                                act.activation(sg[:, u, :], ga[:, u, :], ACT.Silu).then_inc(*silu_made.up)
                            else:
                                act.wait_ge(*hidden_made(f + 1))
                                act.activation(hhi[:, i * 2 + u, :], hs[:, u, :], ACT.Copy).then_inc(*hidden_hi.up)

                    with act.Fori(0, 2 * BT // RAW - 1) as i:
                        gate_up(i, CHUNK)
                    gate_up(2 * BT // RAW - 1, HALF)

                    def down(i, words_last):
                        for j in range(8):
                            words = words_last if j >= 8 - HI else HALF
                            if words:
                                hi_part(c0 + C_DN[b] + i * 8 + j + HI, (j + HI) % RAW, words)
                            if j % 2 and b == NBLK - 1:
                                act.wait_ge(*tile_evac(l * N_TILES + O_DN[b] + i * 4 + j // 2 + 1))
                                square_acc(1, i * 4 + j // 2, j // 2)

                    if b == NBLK - 1:
                        load_sqrt_table()

                    with act.Fori(0, KT // 4 - 1) as i:
                        down(i, HALF)
                    down(KT // 4 - 1, CHUNK if b == 0 else 0)
                make_rms(3)

        @block.vector
        def _(dve):
            dve.memset(epsc[:], EPS).then_inc(*dve_done.up)
            dve.memset(zero[:], 0.0).then_inc(*dve_done.up)
            for c in ahead:
                dve.sem_inc(c.sem, c.head * c.unit)
            dve.wait_ge(*const_landed(3))
            with dve.Fori(0, DEPTH) as l:
                ch = Chain(dve, dve_done, l, DVE_STEPS)
                ch.base = ch.base + 2
                c0, t0 = l * N_CHUNKS, l * N_TILES
                H4, B8, Q = slice(0, MH), BATCH_S, slice(0, MQK)
                sm = slice(SEQ, TOK)

                def lo_part(n, slot, words, spare=False):
                    dve.wait_ge(*hi_made(n + 1))
                    w = slice(0, words)
                    high = whi_spare if spare else whi[:, slot % HI]
                    dve.tensor_tensor(wlo[:, slot, w], raw[:, slot, w], high[:, w].bitcast(F32), ALU.subtract)\
                        .then_inc(*chunk_split.up)

                def operand(gain, m, k):
                    dve.wait_ge(*operand_hi(l * 2 * KT + m * KT + k + 1))
                    dve.scalar_tensor_tensor(out=alo[:, k, :], in0=x[:, k, :], scalar=gains[:, l, gain + k:gain + k + 1],
                                             in1=ahi[:, k, :].bitcast(F32), op0=ALU.mult, op1=ALU.subtract)\
                        .then_inc(*operand_lo.up)

                def make_rstd(e):
                    dve.wait_ge(*rms_made(l * 4 + e + 1))
                    dve.reciprocal(rstd[:], rms[:]).then_inc(*rstd_made.up)
                    dve.wait_ge(*rstd_made(l * 4 + e + 1))

                def scale_acc(gain, k):
                    dve.scalar_tensor_tensor(out=acc[:, k, :], in0=acc[:, k, :], scalar=gains[:, l, gain + k:gain + k + 1],
                                             in1=rstd[:], op0=ALU.mult, op1=ALU.mult).then_inc(*scaled.up)

                def mixed_lo(t, hi, n):
                    return dve.tensor_tensor(mixed[:, t:t + n, :], proj[:, t:t + n, :], mixed[:, hi:hi + n, :].bitcast(F32),
                                             ALU.subtract)

                def rope_tables(_):
                    dve.tensor_tensor(ropes, rope, rstd[:].rearrange("p (o t) -> p o t", o=1).broadcast_to([P, 4, TOK]),
                                      ALU.mult).then_inc(*ropes_made.up)
                    dve.wait_ge(*ropes_made(l + 1))

                def gates_(_):
                    dve.wait_ge(*tile_evac(t0 + 2))
                    dve.tensor_copy(gates[H4, 0, :], proj[MQK:MQK + MH, T_MQ, :])
                    ch(dve.tensor_copy(gates[H4, 1, :], proj[MQK:MQK + MH, T_MQ + 1, :]))
                    dve.tensor_scalar(gates[H4, 0, :], gates[H4, 0, :], gbias[H4, l, 0:1], None, ALU.add)
                    ch(dve.tensor_scalar(gates[H4, 1, :], gates[H4, 1, :], gbias[H4, l, 1:2], None, ALU.add))
                    dve.scalar_tensor_tensor(out=lfa[H4], in0=gates[H4, 1, :], scalar=-1.0, in1=gates[H4, 1, :],
                                             op0=ALU.mult, op1=ALU.min).then_inc(*ml_abs.up)

                def log_f(_):
                    dve.wait_ge(*ml_log(l + 1))
                    ch(dve.scalar_tensor_tensor(out=lfa[H4], in0=gates[H4, 1, :], scalar=0.0, in1=lfb[H4],
                                                op0=ALU.min, op1=ALU.subtract))
                    for c in range(2):
                        t = slice(c * CH, (c + 1) * CH)
                        ins = dve.tensor_tensor_scan(bcum[H4, t], ones[H4, 0:CH], lfa[H4, t], 0.0, ALU.mult, ALU.add)
                    ch(ins)
                    dve.tensor_tensor(gpre[H4, 0:SEQ], gates[H4, 0, 0:SEQ], bcum[H4, 0:SEQ], ALU.subtract)\
                        .then_inc(*ml_rows.up)
                    dve.wait_ge(*ml_rows(l + 1))

                def maxima(_):
                    ch(dve.tensor_tensor_scan(mrun[H4, 0:CH], zero[H4, 0:CH], gpre[H4, 0:CH], 0.0, ALU.add, ALU.max))
                    ch(dve.tensor_tensor(mst[H4, 0:CH], bcum[H4, 0:CH], mrun[H4, 0:CH], ALU.add))
                    ch(dve.tensor_tensor_scan(mrun[H4, CH:SEQ], zero[H4, 0:CH], gpre[H4, CH:SEQ], mst[H4, CH - 1:CH],
                                              ALU.add, ALU.max))
                    ch(dve.tensor_tensor(mst[H4, CH:SEQ], bcum[H4, CH:SEQ], mrun[H4, CH:SEQ], ALU.add))

                def rows(_):
                    dve.tensor_copy(mfin[H4, 0:1], mst[H4, SEQ - 1:SEQ])
                    dve.tensor_scalar(rows1[H4, 0:SEQ], mrun[H4, 0:SEQ], -1.0, None, ALU.mult)
                    dve.tensor_scalar(rows1[H4, SEQ:2 * SEQ], mst[H4, 0:SEQ], -1.0, None, ALU.mult)
                    dve.wait_ge(*m_landed(l + 1))
                    ch(dve.tensor_tensor(bcum[H4, sm], lfa[H4, sm], m0s[H4], ALU.add))
                    ch(dve.tensor_tensor(mss[H4], bcum[H4, sm], gates[H4, 0, sm], ALU.max))
                    dve.tensor_tensor(lft[H4, 0:8], bcum[H4, sm], mss[H4], ALU.subtract)
                    dve.tensor_tensor(lft[H4, 8:16], gates[H4, 0, sm], mss[H4], ALU.subtract)
                    dve.tensor_scalar(lft[H4, 16:24], mss[H4], -1.0, None, ALU.mult).then_inc(*ml_a1.up)

                def scale_keys(_):
                    dve.wait_ge(*tile_evac(t0 + T_MK + MH))
                    keys = proj[Q, T_MK:T_MK + MH, :].rearrange("p a t -> p (a t)")
                    dve.tensor_scalar(keys, keys, MQK ** -0.5, None, ALU.mult).then_inc(*ml_scaled.up)
                    dve.wait_ge(*ml_scaled(l + 1))

                def ml_scores(h):
                    q = l * MH + h
                    dve.wait_ge(*ml_w8(q + 1))
                    ch(dve.tensor_tensor(w8[0:B8], m8[0:B8], ab[0:B8, CH + 8:CH + 16], ALU.mult))
                    dve.tensor_copy(kst[0:B8], bank[6][0:B8, 2 * MQK:3 * MQK])
                    dve.tensor_tensor(aq[Q], proj[Q, T_MQ + h, CH:SEQ], ab[Q, 0:CH], ALU.mult)
                    dve.tensor_tensor(kws[Q], proj[Q, T_MK + h, sm], ab[Q, CH + 8:CH + 16], ALU.mult)
                    if h == 0:
                        dve.wait_ge(*n_landed(l + 1))
                    ch(dve.tensor_tensor(nsn[Q, h, :], nsn[Q, h, :], ab[Q, CH:CH + 8], ALU.mult))
                    ch(dve.tensor_tensor(nsn[Q, h, :], nsn[Q, h, :], kws[Q], ALU.add))
                    dve.tensor_tensor(qn[Q], nsn[Q, h, :], proj[Q, T_MQ + h, sm], ALU.mult)
                    dve.wait_ge(*ml_weights(q + 1))
                    dve.tensor_tensor(msT[:], bank[7][:, 0:SEQ].rearrange("p (c t) -> p c t", c=2), wT[:], ALU.mult)
                    for c in range(2):
                        ins = dve.tensor_scalar(kw[:, c, :], bank[6][:, c * MQK:(c + 1) * MQK], wT[:, c, CH - 1:CH], None, ALU.mult)
                    ins.then_inc(*ml_keys.up)

                def ml_states(h):
                    q = l * MH + h
                    dve.wait_ge(*ml_c1(q + 1))
                    if h:
                        dve.wait_ge(*C2_stored(q))
                    dve.tensor_scalar(nrep[Q], ones[Q], n1[Q, 0:1], None, ALU.mult)
                    dve.scalar_tensor_tensor(out=n2[Q, h:h + 1], in0=n1[Q, 0:1], scalar=ab[Q, CH - 1:CH],
                                             in1=bank[6][Q, 401:402], op0=ALU.mult, op1=ALU.add)
                    dve.scalar_tensor_tensor(out=C2[Q], in0=C1[Q], scalar=ab[Q, CH - 1:CH],
                                             in1=bank[6][Q, MV:2 * MV], op0=ALU.mult, op1=ALU.add).then_inc(*ml_c2.up)
                    dve.wait_ge(*ml_decayed(q + 1))
                    dve.wait_ge(*ml_outer(q + 1))
                    flat = Cs[Q].rearrange("p b v -> p (b v)")
                    for i, bk in enumerate((4, 5, 7)):
                        t = slice(512 * i, 512 * (i + 1))
                        ins = dve.tensor_tensor(flat[:, t], flat[:, t], bank[bk][Q, :], ALU.add)
                    ins.then_inc(*ml_cs.up)

                def ml_outputs(h):
                    q = l * MH + h
                    pair, odd = h // 2, h % 2
                    dve.wait_ge(*ml_num(q + 1))
                    ch(dve.tensor_tensor(en[:], bank[7][:, 0:TOK], en[:], ALU.max))
                    ch(dve.scalar_tensor_tensor(out=en[:], in0=bank[7][:, 0:TOK], scalar=-1.0, in1=en[:],
                                                op0=ALU.mult, op1=ALU.max))
                    ch(dve.reciprocal(en[:], en[:]))
                    half = slice(64 * odd, 64 * odd + 64)
                    dve.tensor_tensor(proj[:, T_MV + 3 * pair + 2 * odd, :], bank[4][:, 0:TOK], en[:], ALU.mult)
                    dve.tensor_tensor(proj[half, T_MV + 3 * pair + 1, :], bank[5][half, 0:TOK], en[half, :], ALU.mult)\
                        .then_inc(*ml_h.up)

                def ml_sum(_):
                    dve.wait_ge(*ml_rms(l + 1))
                    dve.reciprocal(proj[:, 7, :], proj[:, 6, :]).then_inc(*ml_inv.up)

                def ml_norm(_):
                    dve.wait_ge(*ml_spread(l + 1))
                    for h in range(MH):
                        pair, odd = h // 2, h % 2
                        for t, rows_ in ((3 * pair + 2 * odd, slice(0, P)), (3 * pair + 1, slice(64 * odd, 64 * odd + 64))):
                            ins = dve.scalar_tensor_tensor(out=proj[rows_, T_MV + t, :], in0=proj[rows_, T_MV + t, :],
                                                           scalar=gains[rows_, l, G_ML + t:G_ML + t + 1],
                                                           in1=bank[4 + h][rows_, 0:TOK], op0=ALU.mult, op1=ALU.mult)
                    ins.then_inc(*ml_normed.up)
                    dve.wait_ge(*ml_normed(l + 1))

                def ret_scores(h):
                    r = l * RH + h
                    dve.wait_ge(*ret_scored(r + 1))
                    if h == 0:
                        dve.wait_ge(*C2_stored(l * MH + MH))
                        dve.wait_ge(*m_stored(2 * l + 2))
                        dve.wait_ge(*n_stored(2 * l + 2))
                    dve.tensor_tensor(qdec, proj[:, T_RQ(h), CH:SEQ], decq[:, h, :], ALU.mult)
                    dve.tensor_tensor(sT[:], bank[6][:, 0:SEQ].rearrange("p (c t) -> p c t", c=2),
                                      dec[:, h:h + 1, :].broadcast_to([P, 2, CH]), ALU.mult).then_inc(*ret_weighted.up)

                def ret_states(h):
                    r = l * RH + h
                    dve.wait_ge(*ret_s1(r + 1))
                    if h:
                        dve.wait_ge(*S2_stored(r))
                    dve.scalar_tensor_tensor(out=S2, in0=S1, scalar=gchunk[h], in1=bank[7][:, CH:SEQ],
                                             op0=ALU.mult, op1=ALU.add).then_inc(*ret_s2.up)
                    dve.wait_ge(*ret_outer(r + 1))
                    dve.wait_ge(*S_landed[h % 2](l * 3 + h // 2 + 1))
                    for i in range(2):
                        sl = S[:, h % 2, 4 * i:4 * i + 4, :].rearrange("p b v -> p (b v)")
                        ins = dve.scalar_tensor_tensor(out=sl, in0=sl, scalar=gamma[h], in1=bank[4 + i][:, 0:512],
                                                       op0=ALU.mult, op1=ALU.add)
                    ins.then_inc(*ret_snew.up)

                def ret_sum(_):
                    dve.wait_ge(*ret_rms(l + 1))
                    dve.reciprocal(proj[:, 2, :], proj[:, 0, :])
                    dve.reciprocal(proj[0:64, 3, :], proj[0:64, 1, :]).then_inc(*ret_inv.up)

                def ret_norm(part):
                    dve.wait_ge(*ret_spread(2 * l + part + 1))
                    for h in range(4) if part == 0 else (4, 5):
                        ins = dve.scalar_tensor_tensor(out=proj[:, T_RQ(h), :], in0=proj[:, T_RQ(h), :],
                                                       scalar=gains[:, l, G_RET + h:G_RET + h + 1],
                                                       in1=bank[4 + h % 4][:, 0:TOK], op0=ALU.mult, op1=ALU.mult)
                    ins.then_inc(*ret_normed.up)
                    dve.wait_ge(*ret_normed(2 * l + part + 1))

                def ml_split(j):
                    dve.wait_ge(*ml_hi(l * 6 + j + 1))
                    mixed_lo(T_MV + j, T_MO + j, 1)

                def ret_last_product(h):
                    dve.wait_ge(*ret_silu(l * RH + h + 1))
                    y = proj[:, T_RQ(h), :]
                    dve.tensor_tensor(y, y, proj[:, T_RG + h, :], ALU.mult).then_inc(*ret_last_gated.up)
                    dve.wait_ge(*ret_last_gated(l + 1))

                def ret_split(h):
                    dve.wait_ge(*ret_hi(l * RH + h + 1))
                    ins = mixed_lo(T_RQ(h), T_RG + h, 1)
                    if h >= RH - 2:
                        ins.then_inc(*mixed_ready.up)

                def pool_windows(g):
                    win = 2 << g
                    u = proj[:, T_PU + g, :]
                    src = pb if g % 2 == 0 else pa
                    dve.wait_ge(*pl_copied(l * PG + g + 1))
                    ch(dve.tensor_reduce(wsum[:, g, :], pwin[:, g, :, 16 - win:16], AX.X, ALU.add))
                    dve.wait_ge(*plp_stored(l + 1))
                    dve.scalar_tensor_tensor(out=u[:, sm], in0=wsum[:, g, :], scalar=1.0 / win, in1=u[:, sm],
                                             op0=ALU.mult, op1=ALU.subtract)
                    dve.wait_ge(*pl_win(l * PG + g + 1))
                    ch(dve.tensor_tensor(cut16, src[:, 16:32], invc[:, g, :], ALU.mult))
                    dve.tensor_tensor(u[:, 0:16], cut16, u[:, 0:16], ALU.subtract)
                    dve.scalar_tensor_tensor(out=u[:, 16:SEQ], in0=src[:, 32:PW], scalar=1.0 / win, in1=u[:, 16:SEQ],
                                             op0=ALU.mult, op1=ALU.subtract).then_inc(*pl_z.up)

                def pool_split(_):
                    dve.wait_ge(*pl_hi(l + 1))
                    mixed_lo(T_PU, 0, PG)

                steps = {"gates": gates_, "log_f": log_f, "maxima": maxima, "rows": rows, "scale_keys": scale_keys,
                         "ml_scores": ml_scores, "ml_states": ml_states, "ml_outputs": ml_outputs, "ml_sum": ml_sum,
                         "ml_norm": ml_norm, "ret_scores": ret_scores, "ret_states": ret_states, "ret_sum": ret_sum,
                         "ret_norm": ret_norm, "ml_split": ml_split, "ret_last_product": ret_last_product,
                         "ret_split": ret_split, "pool_windows": pool_windows, "pool_split": pool_split,
                         "rope_tables": rope_tables}

                lo_part(c0, 0, CHUNK)
                lo_part(c0 + 1, 1, CHUNK)
                for k in range(KT):
                    operand(G_PREMIX, 0, k)
                make_rstd(0)

                for n in range(NPROJ):
                    dve.wait_ge(*chunk_used(c0 + n + 1))
                    bk = bank[n % BANKS]
                    kind = (n - T_R) % 3 if T_R <= n < T_PU else 0
                    if kind:
                        r2 = l * 2 * RH + 2 * ((n - T_R) // 3) + kind - 1
                        tb = 2 if kind == 1 else 0
                        dve.wait_ge(*rotated(r2))
                        dve.tensor_tensor(rot[:, 0, :], bk[:, 0:TOK], ropes[:, tb, :], ALU.mult)
                        dve.tensor_tensor(rot[64:128, 1, :], bk[0:64, 0:TOK], ropes[0:64, tb + 1, :], ALU.mult)
                        dve.tensor_tensor(rot[0:64, 1, :], bk[64:128, 0:TOK], ropes[64:128, tb + 1, :], ALU.mult)\
                            .then_inc(*tile_evac.up)
                    else:

                        if n == T_PU:
                            dve.wait_ge(*tile_evac(t0 + n))
                        if n == T_MO:
                            dve.wait_ge(*C_stored(l * MH + MH))
                        dve.tensor_tensor(proj[:, n, :], bk[:, 0:TOK], rstd[:], ALU.mult).then_inc(*tile_evac.up)
                    for name, arg in EARLY.get(n, ()):
                        if name in steps:
                            steps[name](arg)
                    lo_part(c0 + n + HI, (n + HI) % RAW, CHUNK)
                    for name, arg in SCHEDULE.get(n, ()):
                        if name in steps:
                            steps[name](arg)

                dve.wait_ge(*S2_stored(l * RH + RH))
                for s in range(2):
                    dve.wait_ge(*S_stored[s](l * 3 + 3))
                dve.wait_ge(*pls_stored(l + 1))
                apart(dve)
                def out_tiles(i, last):
                    for j in range(RAW):
                        dve.wait_ge(*chunk_used(c0 + C_OUT + i * RAW + j + 1))
                        dve.tensor_copy(acc[:, i * RAW + j, :], bank[j][:, 0:TOK]).then_inc(*tile_evac.up)
                        if not last or j < HI:
                            lo_part(c0 + C_OUT + i * RAW + j + HI, (j + HI) % RAW, CHUNK)
                        elif j == HI:
                            lo_part(c0 + C_GU[0], 0, CHUNK)
                            lo_part(c0 + C_GU[0] + 1, 1, CHUNK, spare=True)

                with dve.Fori(0, KT // RAW - 1) as i:
                    out_tiles(i, False)
                out_tiles(KT // RAW - 1, True)
                dve.wait_ge(*tile_evac(t0 + O_OUT + KT))
                make_rstd(1)
                for k in range(KT + LEAD):
                    if k < KT:
                        scale_acc(G_POSTMIX, k)
                    if k >= LEAD:
                        operand(G_PREFFN, 1, k - LEAD)
                make_rstd(2)

                for b in range(NBLK):

                    def gate_up(i, words_last):
                        for j in range(RAW):
                            u = j // 2
                            ahead_ = (c0 + C_GU[b] + i * RAW + j + HI, (j + HI) % RAW, words_last if j >= RAW - HI else CHUNK)
                            dve.wait_ge(*chunk_used(c0 + C_GU[b] + i * RAW + j + 1))
                            f = l * FT + b * BT + i * 2 + u
                            t = t0 + O_GU[b] + i * RAW + j
                            if j % 2 == 0:
                                dve.wait_ge(*silu_made(f - 1))
                                dve.tensor_tensor(ga[:, u, :], bank[j][:, 0:TOK], rstd[:], ALU.mult).then_inc(*tile_evac.up)
                                lo_part(*ahead_)
                            else:
                                dve.tensor_tensor(ua[:, u, :], bank[j][:, 0:TOK], rstd[:], ALU.mult).then_inc(*tile_evac.up)
                                lo_part(*ahead_)
                                dve.wait_ge(*tile_evac(t + 1))
                                dve.wait_ge(*silu_made(f + 1))
                                dve.wait_ge(*hidden_hi(f - 1))
                                dve.tensor_tensor(hs[:, u, :], ua[:, u, :], sg[:, u, :], ALU.mult).then_inc(*hidden_made.up)
                                dve.wait_ge(*hidden_hi(f + 1))
                                dve.wait_ge(*hidden_made(f + 1))
                                dve.tensor_tensor(hlo[:, i * 2 + u, :], hs[:, u, :], hhi[:, i * 2 + u, :].bitcast(F32),
                                                  ALU.subtract).then_inc(*hidden_ready.up)

                    apart(dve)
                    with dve.Fori(0, 2 * BT // RAW - 1) as i:
                        gate_up(i, CHUNK)
                    gate_up(2 * BT // RAW - 1, HALF)

                    def down(i, words_last):
                        for j in range(8):
                            if j % 2:
                                o_, u = i * 4 + j // 2, j // 2
                                dve.wait_ge(*chunk_used(c0 + C_DN[b] + i * 8 + j + 1))
                                if b == 0:
                                    ins = dve.tensor_copy(acc[:, o_, :], bank[u][:, 0:TOK])
                                else:
                                    ins = dve.tensor_tensor(acc[:, o_, :], bank[u][:, 0:TOK], acc[:, o_, :], ALU.add)
                                ins.then_inc(*tile_evac.up)
                            words = words_last if j >= 8 - HI else HALF
                            if words:
                                lo_part(c0 + C_DN[b] + i * 8 + j + HI, (j + HI) % RAW, words)

                    apart(dve)
                    with dve.Fori(0, KT // 4 - 1) as i:
                        down(i, HALF)
                    down(KT // 4 - 1, CHUNK if b == 0 else 0)
                    dve.wait_ge(*tile_evac(t0 + O_DN[b] + KT))
                make_rstd(3)
                for k in range(KT):
                    scale_acc(G_POSTFFN, k)
                ch.close()

        @block.gpsimd
        def _(pool):
            pool.wait_ge(*dve_done(2))
            with pool.Fori(0, DEPTH) as l:
                pch = Chain(pool, pool_done, l, POOL_STEPS)
                Q, B8 = slice(0, MQK), BATCH_S

                def add_square(m, k, slot, first):
                    n = l * 32 + m * KT + k
                    pool.wait_ge(*sq_made(n + 1))
                    pool.wait_ge(*sq_added(n))
                    pool.tensor_tensor(ssq[:], sq[:, slot, :], zero[:] if first else ssq[:], ALU.add).then_inc(*sq_added.up)

                def acc_squares(m):
                    pool.wait_ge(*ssq_summed(l * 2 + m))
                    for j in range(4):
                        add_square(m, j, j, j == 0)
                    apart(pool)
                    with pool.Fori(1, KT // 4) as i:
                        for j in range(4):
                            add_square(m, i * 4 + j, j, False)

                def update_x(m):
                    for k in range(KT):
                        n = l * 2 * KT + m * KT + k
                        pool.wait_ge(*scaled(n + 1))
                        pool.tensor_tensor(x[:, k, :], x[:, k, :], acc[:, k, :], ALU.add).then_inc(*x_updated.up)

                def dma(count, out, in_):
                    apart(pool)
                    pool.dma_start(out, in_).then_inc(*count.up)

                def load_S(h):
                    if h >= 2:
                        pool.wait_ge(*S_stored[h % 2](l * 3 + h // 2))
                        pool.wait_ge(*ret_out(l * RH + h - 1))
                    dma(S_landed[h % 2], S[:, h % 2, :, :], a["s_ret"][l * RH + h])

                def load_C(h):
                    if h:
                        pool.wait_ge(*C_stored(l * MH + h))
                        pool.wait_ge(*ml_num(l * MH + h))
                    dma(C_landed, Cs[Q], a["s_c"][l * MH + h])

                def ml_scores(h):
                    q = l * MH + h
                    pool.wait_ge(*ml_w8(q + 1))
                    pool.wait_ge(*C_landed(q + 1))
                    pool.tensor_tensor(Cs[Q], Cs[Q], ab[Q, CH:CH + 8].rearrange("p (b o) -> p b o", o=1)
                                       .broadcast_to([MQK, B8, MV]), ALU.mult).then_inc(*ml_decayed.up)
                    pool.wait_ge(*ml_keys(q + 1))
                    pool.tensor_tensor(cdiag[0:B8], mvs[0:B8, h * MV:(h + 1) * MV].rearrange("p (o v) -> p o v", o=1)
                                       .broadcast_to([B8, B8, MV]),
                                       w8[0:B8].rearrange("p (b o) -> p b o", o=1).broadcast_to([B8, B8, MV]), ALU.mult)\
                        .then_inc(*ml_diag.up)

                def ml_states(h):
                    q = l * MH + h
                    if h == 0:
                        pool.wait_ge(*ml_a1(l + 1))
                        dma(m_stored, a["m_p"][l], mfin[0:MH, 0:1])
                        dma(m_stored, a["m_s"][l], mss[0:MH])
                    pool.wait_ge(*ml_c2(q + 1))
                    dma(C2_stored, a["c_p"][q], C2[Q])
                    pool.wait_ge(*ml_cs(q + 1))
                    dma(C_stored, a["c_s"][q], Cs[Q])

                def ml_outputs(h):
                    if h + 1 < MH:
                        load_C(h + 1)
                    else:
                        dma(n_stored, a["n_p"][l], n2[Q])
                        dma(n_stored, a["n_s"][l], nsn[Q])

                def ret_scores(h):
                    r = l * RH + h
                    pool.wait_ge(*ret_vks(r + 1))
                    if h == 0:
                        pool.wait_ge(*n_stored(2 * l + 2))
                        pool.wait_ge(*C2_stored(l * MH + MH))
                    pool.tensor_tensor(vdiag[0:B8], vks[0:B8, 0:1, :].broadcast_to([B8, B8, P]),
                                       m8[0:B8].rearrange("p (b o) -> p b o", o=1).broadcast_to([B8, B8, P]), ALU.mult)\
                        .then_inc(*ret_diag.up)
                    if h == 0:
                        apart(pool)
                        pool.memset(pa[:, 0:16], 0.0)
                        pch(pool.memset(pb[:, 0:16], 0.0))
                        dma(pl_landed, pwin[:, :, :, 0:PBUF], a["s_pool"][l])

                def ret_states(h):
                    r = l * RH + h
                    pool.wait_ge(*ret_s2(r + 1))
                    dma(S2_stored, a["ret_p"][r], S2)
                    pool.wait_ge(*ret_snew(r + 1))
                    dma(S_stored[h % 2], a["ret_s"][r], S[:, h % 2, :, :])

                def ret_outputs(h):
                    if h + 2 < RH:
                        load_S(h + 2)

                def pool_windows(g):
                    if g == 0:
                        dma(plp_stored, a["pool_p"][l], proj[:, T_PU:T_PU + PG, SEQ - PBUF:SEQ])
                    pool.wait_ge(*pl_copied(l * PG + g + 1))
                    src, dst = pa, pb
                    for s in range(g + 1):
                        ins = pool.tensor_tensor(dst[:, 16:PW], src[:, 16:PW], src[:, 16 - (1 << s):PW - (1 << s)], ALU.add)
                        if s < g:
                            pch(ins)
                        src, dst = dst, src
                    ins.then_inc(*pl_win.up)
                    if g == PG - 1:
                        dma(pls_stored, a["pool_s"][l], pwin)

                def ml_sigmoid(j):
                    v = proj[:, T_MV + j, :]
                    pool.wait_ge(*ml_sig(l * 6 + j + 1))
                    pool.tensor_tensor(v, v, proj[:, T_MO + j, :], ALU.mult).then_inc(*ml_gated.up)

                def ret_product(h):
                    y = proj[:, T_RQ(h), :]
                    pool.wait_ge(*ret_silu(l * RH + h + 1))
                    pool.wait_ge(*ret_normed(2 * l + h // 4 + 1))
                    pool.tensor_tensor(y, y, proj[:, T_RG + h, :], ALU.mult).then_inc(*ret_gated.up)

                steps = {"ml_scores": ml_scores, "ml_states": ml_states, "ml_outputs": ml_outputs,
                         "ret_scores": ret_scores, "ret_states": ret_states, "ret_outputs": ret_outputs,
                         "pool_windows": pool_windows, "ml_sigmoid": ml_sigmoid, "ret_product": ret_product}

                pool.wait_ge(*pl_y(l))
                dma(wpool_landed, wpool[:], a["w_pool"][l])
                pool.wait_ge(*x_updated(l * 2 * KT))
                dma(m_landed, m0s[0:MH], a["s_m"][l])
                dma(n_landed, nsn[Q], a["s_n"][l])
                load_C(0)
                load_S(0)
                load_S(1)
                for n in range(NPROJ):
                    if T_R <= n < T_PU and (n - T_R) % 3:
                        pool.wait_ge(*tile_evac(l * N_TILES + n + 1))
                        pool.tensor_tensor(proj[:, n, :], rot[:, 0, :], rot[:, 1, :], ALU.add).then_inc(*rotated.up)
                    if n == T_PU + PG:
                        pool.wait_ge(*tile_evac(l * N_TILES + T_PU + PG))
                    for name, arg in SCHEDULE.get(n, ()):
                        if name in steps:
                            steps[name](arg)
                acc_squares(0)
                update_x(0)
                acc_squares(1)
                update_x(1)
                pch.close()
            pool.wait_ge(*m_stored(DEPTH * 2))
            pool.wait_ge(*n_stored(DEPTH * 2))
            pool.wait_ge(*plp_stored(DEPTH))
            pool.wait_ge(*pls_stored(DEPTH))
            pool.wait_ge(*S2_stored(DEPTH * RH))
            pool.wait_ge(*C2_stored(DEPTH * MH))
            pool.wait_ge(*C_stored(DEPTH * MH))
            for s in range(2):
                pool.wait_ge(*S_stored[s](DEPTH * RH // 2))


DVE_STEPS = 42
POOL_STEPS = 7


def kernel(x_prompt, x_sample, state_ret, state_mlstm_c, state_mlstm_n, state_mlstm_m, state_pool,
           w_in, w_out, g_ret_norm, g_mlstm_norm, b_mlstm_i, b_mlstm_f, w_pool, pool_scale,
           g_pre_mix, g_post_mix, g_pre_ffn, g_post_ffn, w_ffn_gate, w_ffn_up, w_ffn_down):
    import concourse.bacc as bacc
    from concourse.bass_utils import run_bass_kernel_spmd

    c = np.ascontiguousarray
    L = DEPTH

    def tiles(w):
        w = np.asarray(w)
        n_in, n_out = w.shape[1] // P, w.shape[2] // P
        return w.reshape(L, n_in, P, n_out, P).transpose(0, 3, 2, 1, 4)

    w_in = np.asarray(w_in)
    rw, mq = RH * RD, MH * MQK
    gate_i = 4 * rw + 2 * mq + 2 * MH * MV
    cols = []
    for part in range(2):
        for h in range(MH):
            s = 4 * rw + part * mq + h * MQK
            t = np.zeros((L, D_MODEL, P), w_in.dtype)
            t[:, :, 0:MQK] = w_in[:, :, s:s + MQK]
            if part == 0 and h < 2:
                t[:, :, MQK:MQK + MH] = w_in[:, :, gate_i + h * MH:gate_i + (h + 1) * MH]
            cols.append(t)
    s = 4 * rw + 2 * mq
    cols.append(w_in[:, :, s:s + MH * MV])
    for h in range(RH):
        for part in (2, 1, 0):
            cols.append(w_in[:, :, part * rw + h * RD:part * rw + (h + 1) * RD])
    cols += [w_in[:, :, gate_i + 2 * MH:], w_in[:, :, s + MH * MV:s + 2 * MH * MV], w_in[:, :, 3 * rw:4 * rw]]
    arrays = {"w_in": c(tiles(np.concatenate(cols, 2)).reshape(L * NPROJ, P, CHUNK)),
              "w_out": c(tiles(w_out).reshape(L * KT, P, CHUNK))}
    gu = np.stack([tiles(w_ffn_gate), tiles(w_ffn_up)], 2)
    arrays["w_gu"] = c(gu.reshape(L * 2 * FT, P, CHUNK))
    dn = np.asarray(w_ffn_down).reshape(L, NBLK, 2, HT, P, KT, P).transpose(0, 1, 5, 2, 4, 3, 6)
    arrays["w_dn"] = c(dn.reshape(L * NBLK * 2 * KT, P, HALF))

    toks = np.concatenate([np.asarray(x_prompt)[0], np.asarray(x_sample)[:, 0]], 0)
    arrays["xT"] = c(toks.reshape(TOK, KT, P).transpose(2, 1, 0))
    table, gamma, gchunk = tables()
    arrays["table"] = table
    by_part = lambda g: np.asarray(g).reshape(L, -1, P).transpose(2, 0, 1)
    arrays["gains"] = c(np.concatenate([by_part(g) for g in (g_pre_mix, g_post_mix, g_pre_ffn, g_post_ffn,
                                                             g_ret_norm, g_mlstm_norm, pool_scale)], 2))
    arrays["w_pool"] = c(np.asarray(w_pool).transpose(0, 2, 1, 3))
    arrays["gbias"] = c(np.stack([np.asarray(b_mlstm_i), np.asarray(b_mlstm_f)], 2).transpose(1, 0, 2))
    arrays["s_ret"] = c(np.asarray(state_ret).transpose(0, 2, 3, 1, 4).reshape(L * RH, RD, BATCH_S, RD))
    arrays["s_c"] = c(np.asarray(state_mlstm_c).transpose(0, 2, 3, 1, 4).reshape(L * MH, MQK, BATCH_S, MV))
    arrays["s_n"] = c(np.asarray(state_mlstm_n).transpose(0, 3, 2, 1))
    arrays["s_m"] = c(np.asarray(state_mlstm_m).transpose(0, 2, 1))
    arrays["s_pool"] = c(np.asarray(state_pool).reshape(L, BATCH_S, PBUF, PG, P).transpose(0, 4, 3, 1, 2))
    outs = {"yT": (P, KT, TOK), "ret_p": (L * RH, RD, RD), "c_p": (L * MH, MQK, MV), "n_p": (L, MQK, MH),
            "m_p": (L, MH, 1), "pool_p": (L, P, PG, PBUF), "ret_s": (L * RH, RD, BATCH_S, RD),
            "c_s": (L * MH, MQK, BATCH_S, MV), "n_s": (L, MQK, MH, BATCH_S), "m_s": (L, MH, BATCH_S),
            "pool_s": (L, P, PG, BATCH_S, 16)}

    nc = bacc.Bacc("TRN2", target_bir_lowering=False, num_devices=1)
    aps = {n: nc.dram_tensor(n, v.shape, F32, kind="ExternalInput").ap() for n, v in arrays.items()}
    aps |= {n: nc.dram_tensor(n, s, F32, kind="ExternalOutput").ap() for n, s in outs.items()}
    build(nc, aps, gamma, gchunk)
    r = run_bass_kernel_spmd(nc, [arrays], core_ids=[0]).results[0]

    y = r["yT"].transpose(2, 1, 0).reshape(TOK, D_MODEL)
    return (c(y[None, 0:SEQ]), c(y[SEQ:, None]),
            c(r["ret_p"].reshape(L, 1, RH, RD, RD)), c(r["c_p"].reshape(L, 1, MH, MQK, MV)),
            c(r["n_p"].transpose(0, 2, 1)[:, None]), c(r["m_p"].reshape(L, 1, MH)),
            c(r["pool_p"].transpose(0, 3, 2, 1).reshape(L, 1, PBUF, PG * P)),
            c(r["ret_s"].reshape(L, RH, RD, BATCH_S, RD).transpose(0, 3, 1, 2, 4)),
            c(r["c_s"].reshape(L, MH, MQK, BATCH_S, MV).transpose(0, 3, 1, 2, 4)),
            c(r["n_s"].transpose(0, 3, 2, 1)), c(r["m_s"].transpose(0, 2, 1)),
            c(r["pool_s"][:, :, :, :, 1:16].transpose(0, 3, 4, 2, 1).reshape(L, BATCH_S, PBUF, PG * P)))
```
